# Optimizing a Trainium2 kernel written in Bass

```python
import math
import jax, jax.numpy as jnp
from jax import lax
import numpy as np

D_MODEL = 1024
BATCH = 1
SEQ = 512
DEPTH = 1

SSD_EXPAND = 2
SSD_D_INNER = SSD_EXPAND * D_MODEL
SSD_HEAD_DIM = 64
SSD_N_HEADS = SSD_D_INNER // SSD_HEAD_DIM
SSD_N_GROUPS = 4
SSD_D_STATE = 128
SSD_CONV = 4
SSD_CHUNK = 128
SSD_CONV_DIM = SSD_D_INNER + 2 * SSD_N_GROUPS * SSD_D_STATE
ATT_HEAD_DIM = 64
ATT_N_HEADS = D_MODEL // ATT_HEAD_DIM
ATT_N_KV = 4
ATT_WINDOW = 128
ATT_BLOCK = 128
ATT_SCALE = ATT_HEAD_DIM ** -0.5
ROPE_THETA = 500000.0
ROPE_DIM = ATT_HEAD_DIM // 4
MOE_N_GROUPS = 8
MOE_EXPERTS_PER_GROUP = 8
MOE_N_EXPERTS = MOE_N_GROUPS * MOE_EXPERTS_PER_GROUP
MOE_TOP_K = 2
MOE_D_FF = 256
MOE_BLOCK = 128
RMS_EPS = 1e-6

COL_Z = SSD_D_INNER
COL_XBC = SSD_CONV_DIM
COL_DT = SSD_N_HEADS
COL_Q = ATT_N_HEADS * ATT_HEAD_DIM
COL_K = ATT_N_KV * ATT_HEAD_DIM
COL_V = ATT_N_KV * ATT_HEAD_DIM
COL_GATE = D_MODEL
IN_COLS = COL_Z + COL_XBC + COL_DT + COL_Q + COL_K + COL_V + 2 * COL_GATE
IN_SPLITS = (COL_Z,
             COL_Z + COL_XBC,
             COL_Z + COL_XBC + COL_DT,
             COL_Z + COL_XBC + COL_DT + COL_Q,
             COL_Z + COL_XBC + COL_DT + COL_Q + COL_K,
             COL_Z + COL_XBC + COL_DT + COL_Q + COL_K + COL_V,
             COL_Z + COL_XBC + COL_DT + COL_Q + COL_K + COL_V + COL_GATE)


def rms_norm(t, g):
    tf = t.astype(jnp.float32)
    tf = tf * lax.rsqrt(jnp.mean(tf * tf, axis=-1, keepdims=True) + RMS_EPS)
    return (tf * g.astype(jnp.float32)).astype(t.dtype)

def ssd_branch(z, xbc, dt_raw, conv_w, conv_b, dt_bias, a_log, d_skip, ssd_norm_g):
    b, s, _ = xbc.shape
    G, J, P, N, L = SSD_N_GROUPS, SSD_N_HEADS // SSD_N_GROUPS, SSD_HEAD_DIM, SSD_D_STATE, SSD_CHUNK
    nc = s // L
    xbc = lax.conv_general_dilated(xbc, conv_w[:, None, :].astype(xbc.dtype), window_strides=(1,),
                                   padding=[(SSD_CONV - 1, 0)], dimension_numbers=('NWC', 'WIO', 'NWC'),
                                   feature_group_count=SSD_CONV_DIM) + conv_b
    xbc = jax.nn.silu(xbc)
    xs, bm, cm = jnp.split(xbc, [SSD_D_INNER, SSD_D_INNER + G * N], axis=-1)
    xs = xs.reshape(b, nc, L, G, J, P)
    bm = bm.reshape(b, nc, L, G, N)
    cm = cm.reshape(b, nc, L, G, N)
    dt = jax.nn.softplus(dt_raw.astype(jnp.float32) + dt_bias.astype(jnp.float32))
    a = -jnp.exp(a_log.astype(jnp.float32))
    dt_c = dt.reshape(b, nc, L, G, J)
    a_cum = jnp.cumsum(dt_c * a.reshape(G, J), axis=2)
    xdt = xs * dt_c[..., None].astype(xs.dtype)
    causal = (jnp.arange(L)[:, None] >= jnp.arange(L)[None, :])[None, None, :, :, None, None]
    seg = a_cum[:, :, :, None] - a_cum[:, :, None, :]
    decay = jnp.exp(jnp.where(causal, seg, -jnp.inf)).astype(xs.dtype)
    cb = jnp.einsum('bclgn,bcsgn->bclsg', cm, bm)
    y_diag = jnp.einsum('bclsgj,bcsgjp->bclgjp', cb[..., None] * decay, xdt)
    decay_to_end = jnp.exp(a_cum[:, :, -1:] - a_cum).astype(xs.dtype)
    states = jnp.einsum('bclgn,bclgjp->bcgjpn', bm, xdt * decay_to_end[..., None])
    chunk_decay = jnp.exp(a_cum[:, :, -1]).astype(states.dtype)

    def step(carry, inp):
        st, dec = inp
        return carry * dec[..., None, None] + st, carry

    init = jnp.zeros((b, G, J, P, N), states.dtype)
    _, prev = lax.scan(step, init, (jnp.moveaxis(states, 1, 0), jnp.moveaxis(chunk_decay, 1, 0)))
    prev = jnp.moveaxis(prev, 0, 1)
    y_off = jnp.einsum('bclgn,bcgjpn->bclgjp', cm, prev) * jnp.exp(a_cum)[..., None].astype(xs.dtype)
    y = (y_diag + y_off + xs * d_skip.reshape(G, J)[:, :, None].astype(xs.dtype)).reshape(b, s, SSD_D_INNER)
    yz = (y * jax.nn.silu(z)).reshape(b, s, G, SSD_D_INNER // G)
    return rms_norm(yz, ssd_norm_g.reshape(G, -1)).reshape(b, s, SSD_D_INNER)

def partial_rope(t, cos, sin):
    half = ROPE_DIM // 2
    t1, t2, rest = t[..., :half], t[..., half:ROPE_DIM], t[..., ROPE_DIM:]
    cos = cos.astype(t.dtype)
    sin = sin.astype(t.dtype)
    return jnp.concatenate([t1 * cos - t2 * sin, t2 * cos + t1 * sin, rest], axis=-1)

def swa_sink_branch(q, k, v, positions, q_norm_g, k_norm_g, sinks):
    b, s, _ = q.shape
    HD, KV, QG, BLK = ATT_HEAD_DIM, ATT_N_KV, ATT_N_HEADS // ATT_N_KV, ATT_BLOCK
    nb = s // BLK
    q = rms_norm(q.reshape(b, s, ATT_N_HEADS, HD), q_norm_g)
    k = rms_norm(k.reshape(b, s, KV, HD), k_norm_g)
    v = v.reshape(b, s, KV, HD)
    inv_freq = ROPE_THETA ** (-jnp.arange(0, ROPE_DIM, 2, dtype=jnp.float32) / ROPE_DIM)
    ang = positions.astype(jnp.float32)[..., None] * inv_freq
    cos, sin = jnp.cos(ang)[:, :, None, :], jnp.sin(ang)[:, :, None, :]
    q = partial_rope(q, cos, sin)
    k = partial_rope(k, cos, sin)
    qb = q.reshape(b, nb, BLK, KV, QG, HD)
    kb = k.reshape(b, nb, BLK, KV, HD)
    vb = v.reshape(b, nb, BLK, KV, HD)
    pad = ((0, 0), (1, 0), (0, 0), (0, 0), (0, 0))
    kk = jnp.concatenate([jnp.pad(kb, pad)[:, :-1], kb], axis=2)
    vv = jnp.concatenate([jnp.pad(vb, pad)[:, :-1], vb], axis=2)
    scores = jnp.einsum('bnqhgd,bnkhd->bnhgqk', qb, kk).astype(jnp.float32) * ATT_SCALE
    qi = jnp.arange(nb)[:, None, None] * BLK + jnp.arange(BLK)[None, :, None]
    ki = (jnp.arange(nb)[:, None, None] - 1) * BLK + jnp.arange(2 * BLK)[None, None, :]
    diff = qi - ki
    mask = (diff >= 0) & (diff < ATT_WINDOW) & (ki >= 0)
    scores = jnp.where(mask[None, :, None, None], scores, -jnp.inf)
    sink = sinks.astype(jnp.float32).reshape(KV, QG)[None, None, :, :, None]
    m = jnp.maximum(jnp.max(scores, axis=-1), sink)
    p = jnp.exp(scores - m[..., None])
    denom = jnp.sum(p, axis=-1) + jnp.exp(sink - m)
    p = (p / denom[..., None]).astype(v.dtype)
    out = jnp.einsum('bnhgqk,bnkhd->bnqhgd', p, vv)
    return out.reshape(b, s, ATT_N_HEADS * HD)

def hier_moe(h2, w_rg, b_rg, w_re, b_re, w_gate_e, w_up_e, w_down_e):
    t = h2.shape[0]
    rows = jnp.arange(t)
    g_logits = jnp.dot(h2, w_rg).astype(jnp.float32) + b_rg.astype(jnp.float32)
    g_prob = jax.nn.softmax(g_logits, axis=-1)
    g_sel = jnp.argmax(g_logits, axis=-1).astype(jnp.int32)
    p_group = g_prob[rows, g_sel]
    e_logits_all = jnp.einsum('td,gde->tge', h2, w_re).astype(jnp.float32) + b_re.astype(jnp.float32)
    e_logits = e_logits_all[rows, g_sel]
    top_v, top_i = lax.top_k(e_logits, MOE_TOP_K)
    gate = p_group[:, None] * jax.nn.softmax(top_v, axis=-1)
    expert_id = g_sel[:, None] * MOE_EXPERTS_PER_GROUP + top_i.astype(jnp.int32)
    n_assign = t * MOE_TOP_K
    flat_e = expert_id.reshape(-1)
    flat_w = gate.reshape(-1)
    flat_t = jnp.arange(n_assign, dtype=jnp.int32) // MOE_TOP_K
    order = jnp.argsort(flat_e)
    sorted_e = flat_e[order]
    counts = jnp.bincount(flat_e, length=MOE_N_EXPERTS)
    starts = jnp.cumsum(counts) - counts
    padded = (counts + MOE_BLOCK - 1) // MOE_BLOCK * MOE_BLOCK
    padded_end = jnp.cumsum(padded)
    padded_start = padded_end - padded
    dest = padded_start[sorted_e] + jnp.arange(n_assign) - starts[sorted_e]
    n_rows = n_assign + MOE_N_EXPERTS * MOE_BLOCK
    n_blocks = n_rows // MOE_BLOCK
    tok = jnp.zeros((n_rows,), jnp.int32).at[dest].set(flat_t[order])
    wt = jnp.zeros((n_rows,), jnp.float32).at[dest].set(flat_w[order])
    block_e = jnp.minimum(jnp.searchsorted(padded_end, jnp.arange(n_blocks) * MOE_BLOCK, side='right'),
                          MOE_N_EXPERTS - 1)
    xs = h2[tok].reshape(n_blocks, MOE_BLOCK, -1)

    def expert_block(args):
        xb, e = args
        hid = jax.nn.silu(xb @ w_gate_e[e]) * (xb @ w_up_e[e])
        return hid @ w_down_e[e]

    ys = lax.map(expert_block, (xs, block_e)).reshape(n_rows, -1)
    return jnp.zeros_like(h2).at[tok].add(ys * wt[:, None].astype(ys.dtype))

def hybrid_layer(x, positions, norm1_g, w_in, conv_w, conv_b, dt_bias, a_log, d_skip, ssd_norm_g,
                 w_ssd_out, q_norm_g, k_norm_g, sinks, w_attn_out, w_out, norm2_g, w_router_group,
                 b_router_group, w_router_expert, b_router_expert, w_gate_e, w_up_e, w_down_e):
    b, s, d = x.shape
    h = rms_norm(x, norm1_g)
    proj = h @ w_in
    z, xbc, dt_raw, q, k, v, g_ssd, g_att = jnp.split(proj, IN_SPLITS, axis=-1)
    y_ssd = ssd_branch(z, xbc, dt_raw, conv_w, conv_b, dt_bias, a_log, d_skip, ssd_norm_g) @ w_ssd_out
    y_att = swa_sink_branch(q, k, v, positions, q_norm_g, k_norm_g, sinks) @ w_attn_out
    merged = jax.nn.sigmoid(g_ssd) * y_ssd + jax.nn.sigmoid(g_att) * y_att
    x = x + merged @ w_out
    h2 = rms_norm(x, norm2_g).reshape(b * s, d)
    y_moe = hier_moe(h2, w_router_group, b_router_group, w_router_expert, b_router_expert,
                     w_gate_e, w_up_e, w_down_e)
    return x + y_moe.reshape(b, s, d)

def first_inputs(seed: int = 0) -> dict:
    key = jax.random.key(seed)
    ks = jax.random.split(key, 24)
    L = DEPTH

    def nrm(k, shape, scale):
        return jax.random.normal(k, shape, jnp.float32) * scale

    x = nrm(ks[0], (BATCH, SEQ, D_MODEL), 1.0)
    positions = (jax.random.randint(ks[1], (BATCH, 1), 0, 1024, dtype=jnp.int32)
                 + jnp.arange(SEQ, dtype=jnp.int32)[None, :])
    dt0 = jnp.exp(jax.random.uniform(ks[6], (L, SSD_N_HEADS), jnp.float32,
                                     minval=math.log(1e-3), maxval=math.log(1e-1)))
    return {
        'x': x,
        'positions': positions,
        'norm1_g': 1.0 + nrm(ks[2], (L, D_MODEL), 0.02),
        'w_in': nrm(ks[3], (L, D_MODEL, IN_COLS), D_MODEL ** -0.5),
        'conv_w': nrm(ks[4], (L, SSD_CONV, SSD_CONV_DIM), SSD_CONV ** -0.5),
        'conv_b': nrm(ks[5], (L, SSD_CONV_DIM), 0.02),
        'dt_bias': dt0 + jnp.log(-jnp.expm1(-dt0)),
        'a_log': jnp.log(jax.random.uniform(ks[7], (L, SSD_N_HEADS), jnp.float32, minval=1.0, maxval=16.0)),
        'd_skip': 1.0 + nrm(ks[8], (L, SSD_N_HEADS), 0.1),
        'ssd_norm_g': 1.0 + nrm(ks[9], (L, SSD_D_INNER), 0.02),
        'w_ssd_out': nrm(ks[10], (L, SSD_D_INNER, D_MODEL), SSD_D_INNER ** -0.5),
        'q_norm_g': 1.0 + nrm(ks[11], (L, ATT_HEAD_DIM), 0.02),
        'k_norm_g': 1.0 + nrm(ks[12], (L, ATT_HEAD_DIM), 0.02),
        'sinks': nrm(ks[13], (L, ATT_N_HEADS), 0.5),
        'w_attn_out': nrm(ks[14], (L, ATT_N_HEADS * ATT_HEAD_DIM, D_MODEL), (ATT_N_HEADS * ATT_HEAD_DIM) ** -0.5),
        'w_out': nrm(ks[15], (L, D_MODEL, D_MODEL), D_MODEL ** -0.5),
        'norm2_g': 1.0 + nrm(ks[16], (L, D_MODEL), 0.02),
        'w_router_group': nrm(ks[17], (L, D_MODEL, MOE_N_GROUPS), D_MODEL ** -0.5),
        'b_router_group': nrm(ks[18], (L, MOE_N_GROUPS), 0.01),
        'w_router_expert': nrm(ks[19], (L, MOE_N_GROUPS, D_MODEL, MOE_EXPERTS_PER_GROUP), D_MODEL ** -0.5),
        'b_router_expert': nrm(ks[20], (L, MOE_N_GROUPS, MOE_EXPERTS_PER_GROUP), 0.01),
        'w_gate_e': nrm(ks[21], (L, MOE_N_EXPERTS, D_MODEL, MOE_D_FF), D_MODEL ** -0.5),
        'w_up_e': nrm(ks[22], (L, MOE_N_EXPERTS, D_MODEL, MOE_D_FF), D_MODEL ** -0.5),
        'w_down_e': nrm(ks[23], (L, MOE_N_EXPERTS, MOE_D_FF, D_MODEL), MOE_D_FF ** -0.5),
    }

def first_block(x, positions, norm1_g, w_in, conv_w, conv_b, dt_bias, a_log, d_skip, ssd_norm_g,
              w_ssd_out, q_norm_g, k_norm_g, sinks, w_attn_out, w_out, norm2_g, w_router_group,
              b_router_group, w_router_expert, b_router_expert, w_gate_e, w_up_e, w_down_e):
    for l in range(DEPTH):
        x = hybrid_layer(x, positions, norm1_g[l], w_in[l], conv_w[l], conv_b[l], dt_bias[l], a_log[l],
                         d_skip[l], ssd_norm_g[l], w_ssd_out[l], q_norm_g[l], k_norm_g[l], sinks[l],
                         w_attn_out[l], w_out[l], norm2_g[l], w_router_group[l], b_router_group[l],
                         w_router_expert[l], b_router_expert[l], w_gate_e[l], w_up_e[l], w_down_e[l])
    return x


DEPTH_2 = 2

N_META = 16
BLOCK_Q = 128
N_A_LAYERS = DEPTH_2 // 2
N_B_LAYERS = DEPTH_2 - N_A_LAYERS
SB_HEADS = 16
SB_HEAD_DIM = D_MODEL // SB_HEADS
DIFF_HEADS = 8
DIFF_QK_DIM = D_MODEL // DIFF_HEADS // 2
DIFF_V_DIM = 2 * DIFF_QK_DIM
ROPE_DIM_2 = DIFF_QK_DIM // 4
D_FF = 4 * D_MODEL
EPS = 1e-6


def rmsnorm(x, g):
    xf = x.astype(jnp.float32)
    y = xf * lax.rsqrt(jnp.mean(xf * xf, axis=-1, keepdims=True) + EPS)
    return (y * g.astype(jnp.float32)).astype(x.dtype)

def rope_tables(T):
    inv_freq = jnp.power(ROPE_THETA, -jnp.arange(0, ROPE_DIM_2, 2, dtype=jnp.float32) / ROPE_DIM_2)
    ang = jnp.arange(T, dtype=jnp.float32)[:, None] * inv_freq[None, :]
    return jnp.cos(ang), jnp.sin(ang)

def apply_partial_rope(x, cos, sin):
    half = ROPE_DIM_2 // 2
    x1 = x[..., :half]
    x2 = x[..., half:ROPE_DIM_2]
    c = cos[:, None, :]
    s = sin[:, None, :]
    return jnp.concatenate([x1 * c - x2 * s, x2 * c + x1 * s, x[..., ROPE_DIM_2:]], axis=-1)

def to_blocks(q):
    B, H, T, D = q.shape
    return q.reshape(B, H, T // BLOCK_Q, BLOCK_Q, D).transpose(2, 0, 1, 3, 4)

def from_blocks(o):
    NB, B, H, BQ, D = o.shape
    return o.transpose(1, 2, 0, 3, 4).reshape(B, H, NB * BQ, D)

def merge_heads(o):
    B, H, T, D = o.shape
    return o.transpose(0, 2, 1, 3).reshape(B, T, H * D)

def stick_breaking_attention(q, k, v):
    T = q.shape[2]
    scale = SB_HEAD_DIM ** -0.5
    kf = k.astype(jnp.float32)
    key_pos = jnp.arange(T)

    def one_block(args):
        qb, q0 = args
        z = jnp.einsum('bhqd,bhkd->bhqk', qb.astype(jnp.float32), kf) * scale
        q_pos = q0 + jnp.arange(BLOCK_Q)
        past = key_pos[None, :] < q_pos[:, None]
        log_keep = jnp.where(past, jax.nn.log_sigmoid(-z), 0.0)
        after = lax.cumsum(log_keep, axis=3, reverse=True) - log_keep
        w = jnp.where(past, jnp.exp(jax.nn.log_sigmoid(z) + after), 0.0)
        return jnp.einsum('bhqk,bhkd->bhqd', w.astype(v.dtype), v)

    starts = jnp.arange(T // BLOCK_Q) * BLOCK_Q
    return from_blocks(lax.map(one_block, (to_blocks(q), starts)))

def differential_attention(q1, q2, k1, k2, v, lam):
    T = q1.shape[2]
    scale = DIFF_QK_DIM ** -0.5
    k1f = k1.astype(jnp.float32)
    k2f = k2.astype(jnp.float32)
    key_pos = jnp.arange(T)

    def one_block(args):
        q1b, q2b, q0 = args
        q_pos = q0 + jnp.arange(BLOCK_Q)
        causal = key_pos[None, :] <= q_pos[:, None]

        def probs(qb, kk):
            s = jnp.einsum('bhqd,bhkd->bhqk', qb.astype(jnp.float32), kk) * scale
            return jax.nn.softmax(jnp.where(causal, s, -jnp.inf), axis=-1)

        w = probs(q1b, k1f) - lam * probs(q2b, k2f)
        return jnp.einsum('bhqk,bhkd->bhqd', w.astype(v.dtype), v)

    starts = jnp.arange(T // BLOCK_Q) * BLOCK_Q
    return from_blocks(lax.map(one_block, (to_blocks(q1), to_blocks(q2), starts)))

def squared_relu_mlp(x, g, w_in, w_out):
    h = rmsnorm(x, g)
    return jnp.square(jax.nn.relu(h @ w_in)) @ w_out

def second_inputs(seed: int = 0) -> dict:
    key = jax.random.key(seed)
    ks = jax.random.split(key, 20)
    nrm = jax.random.normal
    f32 = jnp.float32

    def w(k, shape, fan_in):
        return nrm(k, shape, f32) * fan_in ** -0.5

    def gain(k, shape):
        return 1.0 + 0.05 * nrm(k, shape, f32)

    return {
        "x": nrm(ks[0], (BATCH, SEQ, D_MODEL), f32),
        "meta_tokens": nrm(ks[1], (N_META, D_MODEL), f32),
        "a_norm_g": gain(ks[2], (N_A_LAYERS, D_MODEL)),
        "a_w_qkv": w(ks[3], (N_A_LAYERS, D_MODEL, 3 * D_MODEL), D_MODEL),
        "a_w_o": w(ks[4], (N_A_LAYERS, D_MODEL, D_MODEL), D_MODEL),
        "kv_norm_g": gain(ks[5], (D_MODEL,)),
        "kv_w": w(ks[6], (D_MODEL, DIFF_HEADS * (2 * DIFF_QK_DIM + DIFF_V_DIM)), D_MODEL),
        "kv_k_norm_g": gain(ks[7], (2, DIFF_QK_DIM)),
        "b_norm_g": gain(ks[8], (N_B_LAYERS, D_MODEL)),
        "b_w_q": w(ks[9], (N_B_LAYERS, D_MODEL, DIFF_HEADS * 2 * DIFF_QK_DIM), D_MODEL),
        "b_q_norm_g": gain(ks[10], (N_B_LAYERS, 2, DIFF_QK_DIM)),
        "b_lambda": 0.1 * nrm(ks[11], (N_B_LAYERS, 4, DIFF_QK_DIM), f32),
        "b_subln_g": gain(ks[12], (N_B_LAYERS, DIFF_V_DIM)),
        "b_w_o": w(ks[13], (N_B_LAYERS, DIFF_HEADS * DIFF_V_DIM, D_MODEL), DIFF_HEADS * DIFF_V_DIM),
        "mlp_norm_g": gain(ks[14], (DEPTH_2, D_MODEL)),
        "mlp_w_in": w(ks[15], (DEPTH_2, D_MODEL, D_FF), D_MODEL),
        "mlp_w_out": w(ks[16], (DEPTH_2, D_FF, D_MODEL), D_FF),
    }

def second_block(x, meta_tokens, a_norm_g, a_w_qkv, a_w_o, kv_norm_g, kv_w, kv_k_norm_g,
              b_norm_g, b_w_q, b_q_norm_g, b_lambda, b_subln_g, b_w_o,
              mlp_norm_g, mlp_w_in, mlp_w_out):
    B, S, D = x.shape
    L = S + N_META
    pad = (-L) % BLOCK_Q
    meta = jnp.broadcast_to(meta_tokens.astype(x.dtype)[None], (B, N_META, D))
    h = jnp.concatenate([meta, x, jnp.zeros((B, pad, D), x.dtype)], axis=1)
    T = L + pad
    cos, sin = rope_tables(T)

    shared = None
    for layer in range(DEPTH_2):
        if layer < N_A_LAYERS:
            i = layer
            hn = rmsnorm(h, a_norm_g[i])
            qkv = (hn @ a_w_qkv[i]).reshape(B, T, 3, SB_HEADS, SB_HEAD_DIM)
            q = qkv[:, :, 0].transpose(0, 2, 1, 3)
            k = qkv[:, :, 1].transpose(0, 2, 1, 3)
            v = qkv[:, :, 2].transpose(0, 2, 1, 3)
            o = stick_breaking_attention(q, k, v)
            h = h + merge_heads(o) @ a_w_o[i]
        else:
            j = layer - N_A_LAYERS
            if shared is None:
                kvn = rmsnorm(h, kv_norm_g)
                kv = kvn @ kv_w
                kk = kv[..., :DIFF_HEADS * 2 * DIFF_QK_DIM].reshape(B, T, DIFF_HEADS, 2, DIFF_QK_DIM)
                k1 = apply_partial_rope(rmsnorm(kk[..., 0, :], kv_k_norm_g[0]), cos, sin)
                k2 = apply_partial_rope(rmsnorm(kk[..., 1, :], kv_k_norm_g[1]), cos, sin)
                vv = kv[..., DIFF_HEADS * 2 * DIFF_QK_DIM:].reshape(B, T, DIFF_HEADS, DIFF_V_DIM)
                shared = (k1.transpose(0, 2, 1, 3), k2.transpose(0, 2, 1, 3), vv.transpose(0, 2, 1, 3))
            k1, k2, vv = shared
            lam_init = 0.8 - 0.6 * math.exp(-0.3 * layer)
            lp = b_lambda[j].astype(jnp.float32)
            lam = jnp.exp(jnp.sum(lp[0] * lp[1])) - jnp.exp(jnp.sum(lp[2] * lp[3])) + lam_init
            hn = rmsnorm(h, b_norm_g[j])
            qq = (hn @ b_w_q[j]).reshape(B, T, DIFF_HEADS, 2, DIFF_QK_DIM)
            q1 = apply_partial_rope(rmsnorm(qq[..., 0, :], b_q_norm_g[j, 0]), cos, sin)
            q2 = apply_partial_rope(rmsnorm(qq[..., 1, :], b_q_norm_g[j, 1]), cos, sin)
            o = differential_attention(q1.transpose(0, 2, 1, 3), q2.transpose(0, 2, 1, 3), k1, k2, vv, lam)
            o = rmsnorm(o, b_subln_g[j]) * (1.0 - lam_init)
            h = h + merge_heads(o).astype(h.dtype) @ b_w_o[j]
        h = h + squared_relu_mlp(h, mlp_norm_g[layer], mlp_w_in[layer], mlp_w_out[layer])

    return h[:, N_META:N_META + S]


def setup_inputs(seed=0):
    out = dict(first_inputs(seed))
    for name, value in second_inputs(seed + 1).items():
        if name != "x":
            out[name + "_2"] = value
    return out


def reference(
    x, positions, norm1_g, w_in, conv_w, conv_b, dt_bias, a_log, d_skip, ssd_norm_g, w_ssd_out,
    q_norm_g, k_norm_g, sinks, w_attn_out, w_out, norm2_g, w_router_group, b_router_group,
    w_router_expert, b_router_expert, w_gate_e, w_up_e, w_down_e, meta_tokens_2, a_norm_g_2,
    a_w_qkv_2, a_w_o_2, kv_norm_g_2, kv_w_2, kv_k_norm_g_2, b_norm_g_2, b_w_q_2, b_q_norm_g_2,
    b_lambda_2, b_subln_g_2, b_w_o_2, mlp_norm_g_2, mlp_w_in_2, mlp_w_out_2,
):
    x = first_block(
        x, positions, norm1_g, w_in, conv_w, conv_b, dt_bias, a_log, d_skip, ssd_norm_g,
        w_ssd_out, q_norm_g, k_norm_g, sinks, w_attn_out, w_out, norm2_g, w_router_group,
        b_router_group, w_router_expert, b_router_expert, w_gate_e, w_up_e, w_down_e,
    )
    return second_block(
        x, meta_tokens_2, a_norm_g_2, a_w_qkv_2, a_w_o_2, kv_norm_g_2, kv_w_2, kv_k_norm_g_2,
        b_norm_g_2, b_w_q_2, b_q_norm_g_2, b_lambda_2, b_subln_g_2, b_w_o_2, mlp_norm_g_2,
        mlp_w_in_2, mlp_w_out_2,
    )


_drawn_inputs = setup_inputs


def setup_inputs(seed=0):
    import zlib

    import numpy as np

    out = dict(_drawn_inputs(seed))
    spreads = {}
    factors = {'ssd_norm_g': 2.845,
     'q_norm_g': 8.0,
     'k_norm_g': 7.701,
     'sinks': 64.0,
     'b_router_group': 4.063,
     'b_router_expert': 4.328,
     'kv_norm_g_2': 2.823,
     'kv_k_norm_g_2': 6.59,
     'b_norm_g_2': 5.737,
     'b_q_norm_g_2': 5.703,
     'b_subln_g_2': 3.027}
    for name, (base, spread) in spreads.items():
        noise = np.random.default_rng([zlib.crc32(name.encode()), seed]).standard_normal(out[name].shape)
        drawn = base * np.exp(spread * noise) if base else spread * noise
        out[name] = __import__('jax').numpy.asarray(drawn.astype(out[name].dtype))
    for name, factor in factors.items():
        out[name] = (out[name] * factor).astype(out[name].dtype)
    return out
```

```python
from contextlib import ExitStack

import numpy as np
import concourse.bass as bass
from concourse import mybir

F32 = mybir.dt.float32
F32R = mybir.dt.float32r
I32 = mybir.dt.int32
ACT = mybir.ActivationFunctionType
ALU = mybir.AluOpType
AX = mybir.AxisListType
SET_EXP_LN, SET_TRIG, SET_SILU, SET_SIGMOID = 6, 9, 18, 2
NEG = -1.0e30
T2 = 528
TILES2 = [(0, 128), (128, 256), (256, 384), (384, 512), (512, 528)]
HALVES2 = [(0, 264), (264, 528)]


class Queue:

    def __init__(self, sem):
        self.sem, self.n, self.items, self.met = sem, 0, [], {}

    def wait(self, *marks):
        for m in marks:
            if m is None:
                continue
            if isinstance(m, list):
                self.wait(*m)
                continue
            sem, value = m
            if self.met.get(id(sem), 0) < value:
                self.met[id(sem)] = value
                self.items.append(lambda e, s=sem, v=value: e.wait_ge(s, v))

    def do(self, fn, *marks):
        self.wait(*marks)
        self.n += 1
        self.items.append(lambda e, s=self.sem: fn(e).then_inc(s, 1))
        return self.sem, self.n

    def plain(self, fn, *marks):
        self.wait(*marks)
        self.items.append(fn)

    def mark(self):
        return (self.sem, self.n) if self.n else None

    def emit(self, e):
        for item in self.items:
            item(e)


class Slot:

    def __init__(self, ap, sem=None, free=None):
        self.ap, self.sem, self.n, self.was, self.held = ap, sem, 0, free, False

    @property
    def free(self):
        return self.was

    @free.setter
    def free(self, mark):
        self.was, self.held = mark, False


class Ring:
    def __init__(self, slots):
        self.slots, self.i = slots, 0

    def next(self):
        s = self.slots[self.i % len(self.slots)]
        self.i += 1
        assert not s.held
        s.held = True
        return s


class Later:

    def __init__(self):
        self.units = []

    def push(self, *stages):
        self.units.append(list(stages))

    def tick(self):
        for u in self.units:
            u.pop(0)()
        self.units = [u for u in self.units if u]

    def flush(self):
        while self.units:
            self.tick()


def staged(stages, n, lags=None, old_first=False):
    lags = lags or range(len(stages))
    order = list(zip(stages, lags))
    if old_first:
        order.reverse()
    for step in range(n + lags[-1]):
        for f, lag in order:
            if 0 <= step - lag < n:
                f(step - lag)
        yield


def together(*gens_every):
    live = list(gens_every)
    while live:
        for g in list(live):
            for _ in range(g[1]):
                try:
                    next(g[0])
                except StopIteration:
                    live.remove(g)
                    break


def run_all(g):
    for _ in g:
        pass


class Arena:

    def __init__(self, *tensors):
        self.parts, at = [], 0
        for t in tensors:
            self.parts.append((at, at + t.shape[1], t))
            at += t.shape[1]

    def __getitem__(self, key):
        rows, cols = key
        for a, b, t in self.parts:
            if a <= cols.start and cols.stop <= b:
                return t[rows, cols.start - a:cols.stop - a]
        raise IndexError(cols)


def const_parts():
    p = np.arange(128)
    col = p[None, :]
    row = p[:, None]
    parts = {}
    parts["ident"] = (row == col)
    parts["upto"] = (row <= col)
    parts["before"] = (row < col)
    parts["ones"] = np.ones((128, 128))
    parts["negones"] = -np.ones((128, 128))
    parts["negfrom"] = -(row >= col).astype(np.float32)
    parts["negbig"] = np.where(row > col, NEG, 0.0)
    rot = np.zeros((128, 128))
    for base in (0, 64):
        for m in range(8):
            rot[base + m + 8, base + m] = -1.0
            rot[base + m, base + m + 8] = 1.0
    parts["rot"] = rot
    parts["blk"] = (row // 64 == col // 64) / 64.0
    parts["amask"] = np.concatenate([np.where(col > row, 0.0, NEG), np.where(col <= row, 0.0, NEG)], 1)
    parts["iota64"] = np.broadcast_to(np.arange(64), (128, 64))
    inv = np.float32(500000.0) ** (-np.arange(0, 16, 2, dtype=np.float32) / np.float32(16))
    f = np.zeros((128, 1), np.float32)
    for base in (0, 8, 64, 72):
        f[base:base + 8, 0] = inv
    parts["invf"] = f
    parts["eps"] = np.full((128, 1), 1e-6)
    parts["one"] = np.ones((128, 1))
    return {k: np.ascontiguousarray(v, dtype=np.float32) for k, v in parts.items()}


def const2_parts():
    inv = np.float32(500000.0) ** (-np.arange(0, 16, 2, dtype=np.float32) / np.float32(16))
    ang = np.zeros((128, T2), np.float32)
    for base in (0, 8, 64, 72):
        ang[base:base + 8] = np.arange(T2, dtype=np.float32)[None, :] * inv[:, None]
    return {
        "cos2": np.cos(ang.astype(np.float64)).astype(np.float32),
        "sin2": np.sin(ang.astype(np.float64)).astype(np.float32),
        "iota1024": np.ascontiguousarray(np.broadcast_to(np.arange(1024, dtype=np.float32), (128, 1024))),
    }


SMALL = [("g1", 8), ("g2", 8), ("convw", 96), ("convb", 24), ("ssdg", 16), ("qg", 1), ("kg", 1),
         ("alog", 32), ("dtb", 32), ("dskip", 32), ("sinks", 16), ("rb", 72), ("ang", 8), ("kvg", 8),
         ("bng", 8), ("mg", 16), ("kkg", 1), ("qqg", 1), ("subg", 1), ("lam", 256)]


def small_array(i):
    def cols(v):
        return np.ascontiguousarray(v.reshape(-1, 128).T)

    def rows(v):
        return np.ascontiguousarray(np.broadcast_to(v.reshape(1, -1), (128, v.size)))

    two = lambda v: np.concatenate([v.reshape(64, 1), v.reshape(64, 1)], 0)
    d = {
        "g1": cols(i["norm1_g"]), "g2": cols(i["norm2_g"]),
        "convw": np.ascontiguousarray(i["conv_w"][0].reshape(4, 24, 128).transpose(2, 1, 0)).reshape(128, 96),
        "convb": cols(i["conv_b"]), "ssdg": cols(i["ssd_norm_g"]),
        "qg": two(i["q_norm_g"]), "kg": two(i["k_norm_g"]),
        "alog": rows(i["a_log"]), "dtb": rows(i["dt_bias"]), "dskip": rows(i["d_skip"]),
        "sinks": rows(i["sinks"]),
        "rb": np.concatenate([rows(i["b_router_group"]), rows(i["b_router_expert"])], 1),
        "ang": cols(i["a_norm_g_2"]), "kvg": cols(i["kv_norm_g_2"]), "bng": cols(i["b_norm_g_2"]),
        "mg": np.concatenate([cols(i["mlp_norm_g_2"][0]), cols(i["mlp_norm_g_2"][1])], 1),
        "kkg": i["kv_k_norm_g_2"].reshape(128, 1), "qqg": i["b_q_norm_g_2"].reshape(128, 1),
        "subg": i["b_subln_g_2"].reshape(128, 1), "lam": rows(i["b_lambda_2"]),
    }
    return np.concatenate([d[n] for n, _ in SMALL], 1)


def build(nc, d, out, stop=None, taps=None):
    ctx = ExitStack()
    with ctx:
        def sem(name):
            return ctx.enter_context(nc.semaphore(name))

        NA = 52600
        cp = const_parts()
        nconst = sum(v.shape[1] for v in cp.values())
        nsmall = sum(n for _, n in SMALL)
        n0 = 8 * T2 + nconst + nsmall
        IT = ctx.enter_context(nc.sbuf_tensor("ints", [128, 592], I32))
        PB = [ctx.enter_context(nc.psum_tensor(f"bank{i}", [128, 512], F32)) for i in range(8)]
        A0 = ctx.enter_context(nc.sbuf_tensor("lasting", [128, n0], F32))
        early = ctx.enter_context(ExitStack())
        A = Arena(A0, early.enter_context(nc.sbuf_tensor("early", [128, NA - n0], F32)))
        PE, V, S, G = (Queue(sem(f"s_{n}")) for n in ("pe", "dve", "act", "pool"))
        SP = Queue(sem("s_sp"))
        s_const, s_out, s_x = sem("s_const"), sem("s_out"), sem("s_x")
        slot_sems = [sem(f"s_w{i}") for i in range(9)]
        top = [0]

        def alloc(n):
            o = top[0]
            top[0] += n
            assert top[0] <= NA, top[0]
            return A[:, o:o + n]

        def tiles(k, n):
            return alloc(k * n).rearrange("p (k n) -> p k n", n=n)

        def join():
            marks = [q.mark() for q in (PE, V, S, G)]
            for q in (PE, V, S, G):
                q.wait(*marks)

        def everything():
            return [q.mark() for q in (PE, V, S, G)]

        def dma(dst, src, semaphore, value, *marks):
            SP.wait(*marks)
            SP.items.append(lambda e: e.dma_start(dst, src).then_inc(semaphore, 16))
            return semaphore, value

        def table(n):
            def put(e):
                e.add_instruction(mybir.InstLoadActFuncSet(
                    name=nc.get_next_instruction_name(), engine=mybir.EngineType.Activation,
                    act_func_set_id=n, ins=[], outs=[]))
            S.plain(put)

        def act(o, i, f, *marks, **kw):
            return S.do(lambda e: e.activation(o, i, f, **kw), *marks)

        def tt(q, o, a, b, op, *marks):
            return q.do(lambda e: e.tensor_tensor(o, a, b, op), *marks)

        def ts(q, o, a, s1, s2, op0, op1, *marks):
            if op1 is None:
                return q.do(lambda e: e.tensor_scalar(o, a, s1, None, op0), *marks)
            return q.do(lambda e: e.tensor_scalar(o, a, s1, s2, op0, op1), *marks)

        def stt(o, a, s, b, op0, op1, *marks):
            return V.do(lambda e: e.scalar_tensor_tensor(out=o, in0=a, scalar=s, in1=b, op0=op0, op1=op1), *marks)

        def copy(q, o, a, *marks):
            if q is S:
                return act(o, a, ACT.Copy, *marks)
            return q.do(lambda e: e.tensor_copy(o, a), *marks)

        def reduce(o, a, op, *marks):
            return V.do(lambda e: e.tensor_reduce(o, a, AX.X, op), *marks)

        def mm(o, l, r, start, stop, last=False, *marks):
            f = lambda e: e.matmul(o, l, r, start=start, stop=stop, skip_group_check=True)
            if last:
                return PE.do(f, *marks)
            PE.plain(f, *marks)

        def tr(o, i, last=False, *marks):
            k = i.shape[0]
            f = lambda e: e.transpose(o, i, C["ident"][0:k, 0:k])
            if last:
                return PE.do(f, *marks)
            PE.plain(f, *marks)

        def ring(n, size):
            return Ring([Slot(alloc(size)) for _ in range(n)])

        def bc(ap, n):
            return ap.unsqueeze(len(ap.shape)).to_broadcast([*ap.shape, n])

        def bmid(ap, n):
            return ap.unsqueeze(1).to_broadcast([ap.shape[0], n, ap.shape[1]])

        R = tiles(8, T2)
        C = {}
        call = alloc(nconst)
        o = 0
        for k, v in cp.items():
            C[k] = call[:, o:o + v.shape[1]]
            o += v.shape[1]
        sall = alloc(nsmall)
        o = 0
        for k, n in SMALL:
            C[k] = sall[:, o:o + n]
            o += n
        assert top[0] == n0
        H = tiles(8, T2)
        WN = 4
        W0 = alloc(WN * 2048)
        WR = Ring([Slot(W0[:, i * 2048:(i + 1) * 2048], slot_sems[i]) for i in range(WN)])
        base = top[0]

        BR = Ring([Slot(PB[i]) for i in range(4)])
        XR = Ring([Slot(PB[i]) for i in range(4, 8)])

        def bank(r=None):
            b = (r or BR).next()
            PE.wait(b.free)
            return b

        def wload(view, k0, k1, c0, c1, ring=None):
            s = (ring or WR).next()
            s.n += 16
            n = (k1 - k0) * (c1 - c0)
            dst = s.ap[:, 0:n].rearrange("p (k c) -> p k c", c=c1 - c0)
            src = view[k0 * 128:k1 * 128, c0:c1].rearrange("(k p) c -> p k c", p=128)
            m = dma(dst, src, s.sem, s.n, s.free)
            return dst, m, s

        later = Later()

        def linear_f(view, cols, X, ready, splits, evac, kt=8, r=None):
            per = 2048 // (kt * 128) if kt <= 16 else 1
            i = 0
            while i < len(cols):
                group = [cols[i]]
                while len(group) < per and i + len(group) < len(cols) and cols[i + len(group)] == group[-1] + 128:
                    group.append(cols[i + len(group)])
                chunks = []
                for k0 in range(0, kt, 16):
                    chunks.append(wload(view, k0, min(kt, k0 + 16), group[0], group[-1] + 128))
                for gi, c in enumerate(group):
                    banks = [bank(r) for _ in splits]
                    for ci, (w, m, s) in enumerate(chunks):
                        for k in range(w.shape[1]):
                            kk = ci * 16 + k
                            for b, (n0, n1) in zip(banks, splits):
                                last = k == w.shape[1] - 1 and (n0, n1) == splits[-1]
                                mark = mm(b.ap[:, 0:n1 - n0], w[:, k, gi * 128:gi * 128 + 128], X(kk, n0, n1),
                                          kk == 0, kk == kt - 1, last, m, ready)
                        if gi == len(group) - 1:
                            s.free = mark
                    evac(i + gi, banks, mark)
                    later.tick()
                    yield
                i += len(group)

        def linear_t(view, c0, c1, X, ready, toks, evac, kt=8, r=None):
            for a in range(c0, c1, 256):
                b_ = min(a + 256, c1)
                w, m, s = wload(view, 0, kt, a, b_)
                for ti, (t0, t1) in enumerate(toks):
                    b = bank(r)
                    for k in range(kt):
                        mark = mm(b.ap[0:t1 - t0, 0:b_ - a], X(k, t0, t1), w[:, k, :], k == 0, k == kt - 1,
                                  k == kt - 1, m, ready)
                    if ti == len(toks) - 1:
                        s.free = mark
                    evac(ti, a, b_, b, mark)
                    later.tick()
                    yield

        def norm(X, gains, O, splits, ready, sq, rs):
            for n0, n1 in splits:
                b = bank()
                for k in range(8):
                    s = sq.next()
                    m = act(s.ap[:, 0:n1 - n0], X[:, k, n0:n1], ACT.Square, ready, s.free)
                    s.free = m = mm(b.ap[:, 0:n1 - n0], C["ones"], s.ap[:, 0:n1 - n0], k == 0, k == 7, True, m)
                t = rs.next()
                b.free = act(t.ap[:, 0:n1 - n0], b.ap[:, 0:n1 - n0], ACT.Ln, m, t.free, bias=C["eps"], scale=1.0 / 1024)
                m = act(t.ap[:, 0:n1 - n0], t.ap[:, 0:n1 - n0], ACT.Exp, b.free, scale=-0.5)
                for k in range(8):
                    t.free = stt(O[:, k, n0:n1], X[:, k, n0:n1], gains[:, k:k + 1], t.ap[:, 0:n1 - n0],
                                 ALU.mult, ALU.mult, m)
            return t.free

        def head_norm_rope(b, n, gain, cos, sin, O, bufs, mark):
            st = {}

            def first():
                x, q = st["x"], st["q"] = bufs.next(), bufs.next()
                st["m1"] = copy(S, x.ap[:, 0:n], b.ap[:, 0:n], mark, x.free)
                st["m2"] = b.free = act(q.ap[:, 0:n], b.ap[:, 0:n], ACT.Square, mark, q.free)

            def second():
                x, q = st["x"], st["q"]
                b = bank(XR)
                m = mm(b.ap[:, 0:n], C["blk"], q.ap[:, 0:n], True, True, True, st["m2"])
                m = b.free = act(q.ap[:, 0:n], b.ap[:, 0:n], ACT.Ln, m, bias=C["eps"])
                m = act(q.ap[:, 0:n], q.ap[:, 0:n], ACT.Exp, m, scale=-0.5)
                st["m"] = stt(x.ap[:, 0:n], x.ap[:, 0:n], gain, q.ap[:, 0:n], ALU.mult, ALU.mult, m, st["m1"])

            def third():
                x, q = st["x"], st["q"]
                b = bank(XR)
                m = mm(b.ap[:, 0:n], C["rot"], x.ap[:, 0:n], True, True, True, st["m"])
                m = b.free = tt(V, q.ap[:, 0:n], b.ap[:, 0:n], sin, ALU.mult, m)
                m2 = tt(G, x.ap[:, 0:n], x.ap[:, 0:n], cos, ALU.mult, m)
                x.free = q.free = tt(V, O, x.ap[:, 0:n], q.ap[:, 0:n], ALU.add, m, m2)

            first()
            later.push(lambda: None, second, third)

        dma(call, d["consts"], s_const, 16)
        dma(sall, d["smalls"], s_const, 32)
        dma(IT[:, 0:512], d["pos"], s_const, 48)
        cready = (s_const, 48)
        XT = tiles(4, 1024)
        xready = dma(XT, d["x"].rearrange("a (c p) f -> p (a c) f", p=128), s_x, 16)
        table(SET_TRIG)
        COS, SIN = alloc(512), alloc(512)
        rope_top = top[0]
        t1, t2, t3 = alloc(512), alloc(512), alloc(512)
        KI = A[:, top[0]:top[0] + 512].bitcast(I32)
        alloc(512)

        for k in range(8):
            b = bank()
            PE.wait(cready, xready)
            for c in range(4):
                m = tr(b.ap[:, c * 128:c * 128 + 128], XT[:, c, k * 128:k * 128 + 128], c == 3)
            b.free = copy(V if k % 2 else S, R[:, k, 16:T2], b.ap[:, :], m)
        xm = [V.mark(), S.mark()]
        m = copy(V, t1, IT[:, 0:512], cready)
        m = ts(V, t1, t1, C["invf"], None, ALU.mult, None, m)
        m = ts(V, KI, t1, float(1 / (2 * np.pi)), None, ALU.mult, None, m)
        m = copy(V, t2, KI, m)
        for cst in (6.28125, 0.0019350051879882812, 3.0199159819567e-07):
            m = stt(t1, t2, -cst, t1, ALU.mult, ALU.add, m)
        m = ts(V, t1, t1, 3.1415925, -3.1415925, ALU.min, ALU.max, m)
        m1 = act(SIN, t1, ACT.Sin, m)
        m = ts(V, t1, t1, float(np.pi / 2), None, ALU.add, None, m1)
        m = ts(V, t3, t1, float(np.pi), float(-2 * np.pi), ALU.is_gt, ALU.mult, m)
        m = tt(V, t1, t1, t3, ALU.add, m)
        m = ts(V, t1, t1, 3.1415925, -3.1415925, ALU.min, ALU.max, m)
        rope_ready = act(COS, t1, ACT.Sin, m)
        join()

        top[0] = base
        table(SET_EXP_LN)
        XS = tiles(4, 2048)
        assert top[0] >= base + 8192
        COS2, SIN2 = alloc(512), alloc(512)
        rr = copy(V, COS2, COS, rope_ready)
        rr = copy(V, SIN2, SIN, rope_ready)
        BT = tiles(4, 512)
        CT = tiles(4, 512)
        BK = tiles(4, 512)
        QT = tiles(8, 512)
        KT = tiles(4, 512)
        VT = tiles(4, 256)
        DT = tiles(4, 32)
        DA = tiles(4, 32)
        work = top[0]
        SQ, RS = ring(2, 512), ring(1, 512)
        join()
        h1 = norm(R[:, :, 16:T2], C["g1"], H, [(0, 512)], xm, SQ, RS)
        win = d["w_in"][0]
        Hx = lambda k, a, b: H[:, k, a:b]
        CP = Ring([Slot(alloc(515)) for _ in range(3)])
        for s in CP.slots:
            s.free = V.do(lambda e, a=s.ap: e.memset(a[:, 0:3], 0.0), V.mark())
        CA, CS = ring(2, 512), ring(2, 512)
        table(SET_SILU)

        def evac_xbc(i, banks, mark):
            b = banks[0]
            s, a = CP.next(), CA.next()
            m = b.free = copy(S, s.ap[:, 3:515], b.ap[:, :], mark, s.free)
            w = C["convw"]
            m = ts(V, a.ap, s.ap[:, 3:515], w[:, 4 * i + 3:4 * i + 4], None, ALU.mult, None, m, a.free)
            for j in (2, 1, 0):
                m = stt(a.ap, s.ap[:, j:j + 512], w[:, 4 * i + j:4 * i + j + 1], a.ap, ALU.mult, ALU.add, m)
            s.free = m
            if i < 16:
                o = CS.next()
                dst = o.ap
            else:
                o = None
                dst = (BT if i < 20 else CT)[:, (i - 16) % 4, :]
            m = act(dst, a.ap, ACT.Silu, m, o.free if o else None, bias=C["convb"][:, i:i + 1])
            a.free = m

            def transposes():
                if i >= 20:
                    return
                b = bank(XR)
                for c in range(4):
                    mt = tr(b.ap[:, c * 128:c * 128 + 128], dst[:, c * 128:c * 128 + 128], c == 3, m)
                if o:
                    o.free = mt
                    D_ = XS[:, :, i * 128:i * 128 + 128]
                else:
                    D_ = BK[:, :, (i - 16) * 128:(i - 15) * 128]
                b.free = copy(V if i % 2 else S, D_, b.ap[:, :].rearrange("p (c n) -> p c n", n=128), mt)
            later.push(lambda: None, transposes)

        run_all(linear_f(win, [2048 + 128 * i for i in range(24)], Hx, h1, [(0, 512)], evac_xbc))
        later.flush()
        TOK = [(c * 128, c * 128 + 128) for c in range(4)]

        bD = bank()
        w, m, s = wload(win, 0, 8, 5120, 5152)
        for c in range(4):
            for k in range(8):
                mk = mm(bD.ap[:, c * 32:c * 32 + 32], H[:, k, c * 128:c * 128 + 128], w[:, k, :], k == 0, k == 7,
                        k == 7, m)
        s.free = mk
        join()
        top[0] = work
        table(SET_EXP_LN)
        NAC, EAC, DTE, CDC = tiles(4, 32), tiles(4, 32), tiles(4, 32), tiles(4, 32)
        work2 = top[0]
        dx, du, dw, dl = alloc(128), alloc(128), alloc(128), alloc(128)
        v3 = lambda a: a.rearrange("p (c n) -> p c n", n=32)
        m = tt(V, v3(dx), v3(bD.ap[:, 0:128]), bmid(C["dtb"], 4), ALU.add, mk)
        bD.free = m
        m = ts(V, du, dx, 40.0, None, ALU.min, None, m)
        m = act(du, du, ACT.Exp, m)
        m = ts(V, dw, du, 1.0, None, ALU.add, None, m)
        m1 = act(dl, dw, ACT.Ln, m)
        m = ts(V, dw, dw, -1.0, 1e-30, ALU.add, ALU.max, m1)
        m = V.do(lambda e: e.reciprocal(dw, dw), m)
        m = tt(V, dl, dl, du, ALU.mult, m, m1)
        m = tt(V, dl, dl, dw, ALU.mult, m)
        m = tt(V, v3(dl), v3(dl), v3(dx), ALU.max, m)
        mdt = copy(V, DT, v3(dl), m)
        ea = alloc(32)
        m = act(ea, C["alog"], ACT.Exp)
        m = stt(DA, DT, -1.0, bmid(ea, 4), ALU.mult, ALU.mult, m, mdt)
        bA, bB = bank(), bank()
        for c in range(4):
            mk1 = mm(bA.ap[:, c * 32:c * 32 + 32], C["upto"], DA[:, c, :], True, True, True, m)
            mk2 = mm(bB.ap[:, c * 32:c * 32 + 32], C["ones"], DA[:, c, :], True, True, True, m)
        m1 = ts(V, NAC, v3(bA.ap[:, 0:128]), -1.0, None, ALU.mult, None, mk1, mk2)
        m = tt(V, DTE, v3(bB.ap[:, 0:128]), NAC, ALU.add, m1)
        act(EAC, v3(bA.ap[:, 0:128]), ACT.Exp, mk1, m1)
        act(DTE, DTE, ACT.Exp, m)
        bA.free = bB.free = act(CDC, v3(bB.ap[:, 0:128]), ACT.Exp, mk2, m)
        dt_ready = [S.mark(), V.mark()]

        HB = ring(8, 512)

        def evac_k(i, banks, mark):
            head_norm_rope(banks[0], 512, C["kg"], COS2, SIN2, KT[:, i, :], HB, mark)

        def evac_q(i, banks, mark):
            head_norm_rope(banks[0], 512, C["qg"], COS2, SIN2, QT[:, i, :], HB, mark)

        def evac_v(ti, a, b_, b, mark):
            b.free = copy(V, VT[:, ti, :], b.ap[:, 0:256], mark)

        wk, m, s = wload(win, 0, 8, 6176, 6432)
        for i in range(4):
            b = bank()
            for k in range(8):
                l = wk[:, k, i * 64:i * 64 + 64]
                for half in (0, 1):
                    mk = mm(b.ap[64 * half:64 * half + 64, :], l, H[:, k, 0:512], k == 0, k == 7, k == 7 and half == 1, m)
            evac_k(i, [b], mk)
            later.tick()
        s.free = mk
        run_all(linear_f(win, [5152 + 128 * i for i in range(8)], Hx, h1, [(0, 512)], evac_q))
        run_all(linear_t(win, 6432, 6688, Hx, h1, TOK, evac_v))
        later.flush()
        join()

        if stop == "qkv":
            taps.update({"XS": XS, "BT": BT, "CT": CT, "QT": QT, "KT": KT, "VT": VT, "DT": DT, "H": H[:, :, 0:512], "COS": COS2, "SIN": SIN2, "EAC": EAC, "DTE": DTE, "CDC": CDC})
            return finish(nc, locals())

        top[0] = work2
        cb, EX, XD, XE, TM = ring(1, 128), ring(2, 1024), ring(2, 512), ring(2, 512), ring(1, 512)
        ST = ring(2, 512)
        SSQ = alloc(16)
        h8 = lambda a: a.rearrange("p (j n) -> p j n", j=8)
        ydone = {}

        def ssd():
            units = [(g, c) for g in range(4) for c in range(4)]
            u = {}

            def s0(i):
                g, c = units[i]
                t = u[i] = {}
                cs = slice(c * 128, c * 128 + 128)
                t["bc"] = b = bank(XR)
                m = mm(b.ap[:, 0:128], BT[:, g, cs], CT[:, g, cs], True, True, True)
                t["cb"] = q = cb.next()
                t["mcb"] = b.free = copy(V, q.ap, b.ap[:, 0:128], m, q.free)
                t["e"] = e_ = EX.next()
                for half in range(2):
                    b = bank(XR)
                    mm(b.ap[:, :].rearrange("p (j n) -> p j n", j=4),
                       C["ident"], bmid(C["negbig"], 4), True, False)
                    for j in range(4):
                        h = g * 8 + half * 4 + j
                        m = mm(b.ap[:, j * 128:j * 128 + 128], DA[:, c, h:h + 1].to_broadcast([128, 128]),
                               C["upto"], False, j == 3, j == 3, dt_ready)
                    for j in range(4):
                        h = g * 8 + half * 4 + j
                        jj = half * 4 + j
                        t["me"] = b.free = act(e_.ap[:, jj * 128:jj * 128 + 128], b.ap[:, j * 128:j * 128 + 128], ACT.Exp,
                                               m, e_.free, dt_ready, bias=NAC[:, c, h:h + 1])
                hs = slice(g * 8, g * 8 + 8)
                fs = slice(g * 512, g * 512 + 512)
                t["xd"], t["xe"] = XD.next(), None
                t["mxd"] = tt(G, h8(t["xd"].ap), h8(XS[:, c, fs]), bc(DT[:, c, hs], 64), ALU.mult, t["xd"].free, dt_ready)
                if c < 3:
                    t["xe"] = XE.next()
                    t["mxe"] = tt(G, h8(t["xe"].ap), h8(t["xd"].ap), bc(DTE[:, c, hs], 64), ALU.mult, t["xe"].free, t["mxd"])
                t["msk"] = tt(G, h8(XS[:, c, fs]), h8(XS[:, c, fs]), bc(C["dskip"][:, hs], 64), ALU.mult, t["mxd"])
                t["m"] = tt(V, h8(e_.ap), h8(e_.ap), bmid(t["cb"].ap, 8), ALU.mult, t["me"], t["mcb"])
                t["cb"].free = t["m"]

            def s1(i):
                g, c = units[i]
                t = u[i]
                cs = slice(c * 128, c * 128 + 128)
                hs = slice(g * 8, g * 8 + 8)
                fs = slice(g * 512, g * 512 + 512)
                b = bank(XR)
                for j in range(8):
                    m = mm(b.ap[:, j * 64:j * 64 + 64], t["e"].ap[:, j * 128:j * 128 + 128],
                           t["xd"].ap[:, j * 64:j * 64 + 64], True, True, j == 7, t["m"], t["mxd"])
                t["e"].free = t["xd"].free = m
                y = XS[:, c, fs]
                my = b.free = tt(V, y, y, b.ap[:, :], ALU.add, m, t["msk"])
                if c > 0:
                    st, mst = u["st"]
                    b = bank(XR)
                    m = mm(b.ap[:, :], CT[:, g, cs], st.ap, True, True, True, mst)
                    st.free = m
                    w_ = TM.next()
                    m = b.free = tt(V, h8(w_.ap), h8(b.ap[:, :]), bc(EAC[:, c, hs], 64), ALU.mult, m, w_.free)
                    my = w_.free = tt(V, y, y, w_.ap, ALU.add, m, my)
                ydone[g, c] = my
                if c < 3:
                    b = bank(XR)
                    m = mm(b.ap[:, :], BK[:, c, g * 128:g * 128 + 128], t["xe"].ap, True, True, True, t["mxe"])
                    t["xe"].free = m
                    nx = ST.next()
                    if c == 0:
                        mn = b.free = copy(V, nx.ap, b.ap[:, :], m, nx.free)
                    else:
                        st, mst = u["st"]
                        m2 = tt(V, h8(nx.ap), h8(st.ap), bc(CDC[:, c, hs], 64), ALU.mult, nx.free, mst)
                        mn = b.free = tt(V, nx.ap, nx.ap, b.ap[:, :], ALU.add, m, m2)
                        st.free = [st.free, m2]
                    u["st"] = (nx, mn)

            yield from staged([s0, s1], 16)

        SB, PT = ring(2, 1024), ring(2, 1024)
        VEC = ring(3, 16)
        ZR = ring(2, 256)

        def attention():
            units = [(n, kv) for n in range(4) for kv in range(4)]
            u = {}

            def a0(i):
                n, kv = units[i]
                t = u[i] = {}
                w = 256 if n else 128
                k0 = (n - 1) * 128 if n else 0
                t["s"] = s = SB.next()
                sv = s.ap[:, 0:4 * w].rearrange("p (h k) -> p h k", k=w)
                msk = C["amask"][:, 256 - w:256]
                for bb in range(2):
                    b = bank(XR)
                    pr = slice(bb * 64, bb * 64 + 64)
                    for hh in range(2):
                        h = kv * 4 + 2 * hh + bb
                        m = mm(b.ap[:, hh * w:hh * w + w], QT[pr, h // 2, n * 128:n * 128 + 128],
                               KT[pr, kv, k0:k0 + w], True, True, hh == 1)
                    bv = b.ap[:, 0:2 * w].rearrange("p (h k) -> p h k", k=w)
                    m = b.free = stt(sv[:, bb * 2:bb * 2 + 2, :], bv, 0.125, bmid(msk, 2), ALU.mult, ALU.add, m, s.free)
                q = t["v"] = VEC.next()
                m = reduce(q.ap[:, 0:4], sv, ALU.max, m, q.free)
                sk = C["sinks"][:, kv * 4:kv * 4 + 4].rearrange("p (a b) -> p b a", b=2)
                q2 = lambda i: q.ap[:, i:i + 4].rearrange("p (b a) -> p b a", b=2)
                m = tt(V, q2(0), q2(0), sk, ALU.max, m)
                m1 = tt(V, q2(12), sk, q2(0), ALU.subtract, m)
                m = ts(V, q.ap[:, 4:8], q.ap[:, 0:4], -1.0, None, ALU.mult, None, m)
                m1 = act(q.ap[:, 12:16], q.ap[:, 12:16], ACT.Exp, m1)
                for j in range(4):
                    m2 = act(sv[:, j, :], sv[:, j, :], ACT.Exp, m, bias=q.ap[:, 4 + j:5 + j], accum_out=q.ap[:, 8 + j:9 + j])
                m = tt(V, q.ap[:, 8:12], q.ap[:, 8:12], q.ap[:, 12:16], ALU.add, m1, m2)
                m = V.do(lambda e: e.reciprocal(q.ap[:, 8:12], q.ap[:, 8:12]), m)
                t["ms"] = q.free = tt(G, sv, sv, bc(q.ap[:, 8:12], w), ALU.mult, m)

            def a1(i):
                n, kv = units[i]
                t = u[i]
                w = 256 if n else 128
                s = t["s"]
                p = t["p"] = PT.next()
                nb = 4 * w // 512
                for bb in range(nb):
                    b = bank(XR)
                    for j in range(4):
                        c = (bb * 4 + j) * 128
                        m = tr(b.ap[:, j * 128:j * 128 + 128], s.ap[:, c:c + 128], j == 3, t["ms"])
                    t["mp"] = b.free = copy(S if bb else V, p.ap[:, bb * 512:bb * 512 + 512], b.ap[:, :], m, p.free)
                    t.setdefault("mps", []).append(b.free)
                s.free = m

            def a2(i):
                n, kv = units[i]
                t = u[i]
                p = t["p"]
                w = 256 if n else 128
                b = bank(XR)
                nk = w // 128
                pv = p.ap[:, 0:4 * w].rearrange("p (b a k n) -> p b a k n", b=2, a=2, n=128)
                for kk in range(nk):
                    for bb in range(2):
                        m = mm(b.ap[64 * bb:64 * bb + 64, 0:256].rearrange("p (a n) -> p a n", n=128),
                               VT[:, n - nk + 1 + kk, kv * 64:kv * 64 + 64], pv[:, bb, :, kk, :],
                               kk == 0, kk == nk - 1, bb == 1 and kk == nk - 1, t["mps"])
                p.free = m
                b.free = copy(S, QT[:, kv * 2:kv * 2 + 2, n * 128:n * 128 + 128],
                              b.ap[:, 0:256].rearrange("p (a n) -> p a n", n=128), m)

            yield from staged([a0, a1, a2], 16, (0, 1, 2), True)


        def evac_z(ti, a, b_, b, mark):
            z = ZR.next()
            m = ts(V, z.ap, b.ap[:, 0:256], -80.0, None, ALU.max, None, mark, z.free)
            m = act(z.ap, z.ap, ACT.Exp, m, scale=-1.0)
            m = ts(V, z.ap, z.ap, 1.0, None, ALU.add, None, m)
            m = V.do(lambda e: e.reciprocal(z.ap, z.ap), m)
            m = b.free = tt(V, z.ap, z.ap, b.ap[:, 0:256], ALU.mult, m)
            y = XS[:, ti, a:b_]
            z.free = tt(G, y, y, z.ap, ALU.mult, m, ydone[a // 512, ti])

        def zs():
            for _ in range(8):
                yield
            yield from linear_t(win, 0, 2048, Hx, h1, TOK, evac_z)

        together((ssd(), 1), (attention(), 1), (zs(), 2))
        later.flush()
        join()
        if stop == "y":
            taps.update({"XS": XS, "AT": QT})
            join()
            return finish(nc, locals())
        join()

        top[0] = work2
        SQ = ring(2, 512)
        for c in range(4):
            for g in range(4):
                q = SQ.next()
                m = q.free = act(q.ap, XS[:, c, g * 512:g * 512 + 512], ACT.Square, q.free,
                                 accum_out=SSQ[:, c * 4 + g:c * 4 + g + 1])
        m = act(SSQ, SSQ, ACT.Ln, m, bias=C["eps"], scale=1.0 / 512)
        m = act(SSQ, SSQ, ACT.Exp, m, scale=-0.5)
        ms = {}
        for c in range(4):
            for g in range(4):
                y = XS[:, c, g * 512:g * 512 + 512]
                ms[c, g] = ts(V, y, y, SSQ[:, c * 4 + g:c * 4 + g + 1], None, ALU.mult, None, m)
        join()
        AT = QT
        top[0] = work2
        lo = base + 8192 + 1024
        YA = A[:, lo:lo + 4096 + 2048].rearrange("p (k n) -> p k n", n=512)
        YB = tiles(4, 512)
        M8 = tiles(8, 512)
        ysl = [YA[:, k, :] for k in range(12)] + [YB[:, k, :] for k in range(4)]
        GT = ring(4, 512)
        for ft in range(16):
            b = bank(XR)
            for c in range(4):
                m = tr(b.ap[:, c * 128:c * 128 + 128], XS[:, c, ft * 128:ft * 128 + 128], c == 3)
            if ft % 2:
                b.free = act(ysl[ft], b.ap[:, :], ACT.Copy, m, scale=C["ssdg"][:, ft:ft + 1])
            else:
                b.free = ts(V, ysl[ft], b.ap[:, :], C["ssdg"][:, ft:ft + 1], None, ALU.mult, None, m)
        yz = [S.mark(), V.mark()]
        table(SET_SIGMOID)
        gates = {}

        def evac_gate(name):
            def f(i, banks, mark):
                t = GT.next()
                banks[0].free = act(t.ap, banks[0].ap[:, :], ACT.Sigmoid, mark, t.free)
                gates[name, i] = t, banks[0].free
            return f

        def evac_sum(name, first):
            def f(i, banks, mark):
                t, m = gates[name, i]
                if first:
                    banks[0].free = t.free = tt(V, M8[:, i, :], banks[0].ap[:, :], t.ap, ALU.mult, mark, m)
                else:
                    banks[0].free = m = tt(V, t.ap, banks[0].ap[:, :], t.ap, ALU.mult, mark, m)
                    t.free = tt(V, M8[:, i, :], M8[:, i, :], t.ap, ALU.add, m)
            return f

        cs = [128 * i for i in range(8)]
        gs = linear_f(win, [6688 + c for c in cs], Hx, h1, [(0, 512)], evac_gate("s"))
        ga = linear_f(win, [7712 + c for c in cs], Hx, h1, [(0, 512)], evac_gate("a"))
        ys = linear_f(d["w_ssd_out"][0], cs, lambda k, a, b: ysl[k], yz, [(0, 512)], evac_sum("s", True), kt=16)
        ya = linear_f(d["w_attn_out"][0], cs, lambda k, a, b: AT[:, k, :], None, [(0, 512)], evac_sum("a", False))
        for i in range(4):
            for g in (gs, ys, ga, ya):
                next(g, None)
                next(g, None)
        for g in (gs, ys, ga, ya):
            run_all(g)
        mg = V.mark()

        def evac_res(i, banks, mark):
            r = R[:, i, 16:T2]
            banks[0].free = tt(V, r, r, banks[0].ap[:, :], ALU.add, mark)

        run_all(linear_f(d["w_out"][0], cs, lambda k, a, b: M8[:, k, :], mg, [(0, 512)], evac_res))
        join()
        if stop == "x1":
            taps.update({"R": R[:, :, 16:T2], "M8": M8})
            return finish(nc, locals())

        table(SET_EXP_LN)
        top[0] = base
        WX = Ring([WR.slots[i] for i in range(WN)] + [Slot(alloc(2048), slot_sems[WN + i], everything()) for i in range(3)])
        XSO = tiles(8, 1536)
        YSO = tiles(8, 1536)
        XW = H[:, :, 0:512]
        ytop = base + 3 * 2048 + 12288
        save = top[0]
        top[0] = ytop
        HT = tiles(4, 1024)
        PM = tiles(4, 1024)
        IO = alloc(1024)
        SQ, RS = ring(2, 512), ring(1, 512)
        assert top[0] <= ytop + 12288
        top[0] = save

        LG = tiles(4, 72)
        small = alloc(256 * 4)
        OH1, OH2, E64, T64 = (small[:, i * 256:i * 256 + 256].rearrange("p (c e) -> p c e", e=64) for i in range(4))
        g8 = tiles(4, 8)
        g8b = tiles(4, 8)
        sc = alloc(64)
        col = lambda i: sc[:, 4 * i:4 * i + 4]
        CNT, STR, ONE64 = alloc(64), alloc(64), alloc(64)
        D1, D2, W1, W2 = (alloc(4) for _ in range(4))
        mio = dma(IO, d["iota1024"], s_x, 32, everything())
        RWt = A[:, top[0]:top[0] + 576].rearrange("p (k n) -> p k n", n=72)
        alloc(576)
        mrw = dma(RWt, d["rw"].rearrange("(k p) n -> p k n", p=128), s_x, 48, everything())
        mio = mrw = (s_x, 48)
        h2 = norm(R[:, :, 16:T2], C["g2"], H, [(0, 512)], None, SQ, RS)
        b = bank()
        for c in range(4):
            for k in range(8):
                m = mm(b.ap[:, c * 72:c * 72 + 72], H[:, k, c * 128:c * 128 + 128], RWt[:, k, :], k == 0, k == 7,
                       k == 7, h2, mrw)
        m = b.free = tt(V, LG, b.ap[:, 0:288].rearrange("p (c n) -> p c n", n=72), bmid(C["rb"], 4), ALU.add, m)
        for k in range(4):
            for q in range(2):
                b = bank()
                for j in range(4):
                    f = q * 4 + j
                    mk = tr(b.ap[:, j * 128:j * 128 + 128], H[:, f, k * 128:k * 128 + 128], j == 3, h2)
                b.free = copy(S, HT[:, k, q * 512:q * 512 + 512], b.ap[:, :], mk)
        hts = S.mark()

        def vv(fn):
            return V.do(fn, V.mark())

        def argfirst(values, n, mx, oh, tmp, idx):
            io = C["iota64"][:, 0:n]
            tt(V, oh, values, bc(mx, n), ALU.is_ge, V.mark())
            ts(V, oh, oh, -1000.0, 1000.0, ALU.mult, ALU.add, V.mark())
            tt(V, tmp, oh, bmid(io, 4), ALU.add, V.mark())
            reduce(idx, tmp, ALU.min, V.mark())
            return tt(V, oh, bmid(io, 4), bc(idx, n), ALU.is_equal, V.mark())

        gl = LG[:, :, 0:8]
        reduce(col(0), gl, ALU.max, V.mark())
        argfirst(gl, 8, col(0), g8, g8b, col(1))
        m = tt(V, g8b, gl, bc(col(0), 8), ALU.subtract, V.mark())
        m = act(g8b, g8b, ACT.Exp, m)
        reduce(col(2), g8b, ALU.add, m)
        vv(lambda e: e.reciprocal(col(2), col(2)))
        ts(V, g8, g8, -NEG, NEG, ALU.mult, ALU.add, V.mark())
        for c in range(4):
            tt(V, E64[:, c, :].rearrange("p (g e) -> p g e", e=8), LG[:, c, 8:72].rearrange("p (g e) -> p g e", e=8),
               bc(g8[:, c, :], 8), ALU.add, V.mark())
        reduce(col(3), E64, ALU.max, V.mark())
        argfirst(E64, 64, col(3), OH1, T64, col(1))
        stt(E64, OH1, NEG, E64, ALU.mult, ALU.add, V.mark())
        reduce(col(4), E64, ALU.max, V.mark())
        argfirst(E64, 64, col(4), OH2, T64, col(1))
        m = tt(V, col(5), col(4), col(3), ALU.subtract, V.mark())
        m = act(col(5), col(5), ACT.Exp, m)
        ts(V, col(6), col(5), 1.0, None, ALU.add, None, m)
        vv(lambda e: e.reciprocal(col(6), col(6)))
        tt(V, W1, col(6), col(2), ALU.mult, V.mark())
        tt(V, W2, W1, col(5), ALU.mult, V.mark())
        mo = tt(V, T64, OH1, OH2, ALU.add, V.mark())
        b, b2 = bank(), bank()
        for c in range(4):
            for j in range(c + 1):
                mk = mm(b.ap[:, c * 64:c * 64 + 64], C["before"] if j == c else C["ones"], T64[:, j, :], j == 0, j == c,
                        j == c, mo)
            mk = mm(b2.ap[:, 0:64], C["ones"], T64[:, c, :], c == 0, c == 3, c == 3, mo)
        m = copy(V, CNT, b2.ap[:, 0:64], mk)
        m = V.do(lambda e: e.memset(ONE64, 1.0), m)
        m = V.do(lambda e: e.tensor_tensor_scan(STR, ONE64, CNT, 0.0, ALU.mult, ALU.add), m)
        m = b2.free = tt(V, STR, STR, CNT, ALU.subtract, m)
        m = b.free = tt(V, E64, b.ap[:, 0:256].rearrange("p (c n) -> p c n", n=64), bmid(STR, 4), ALU.add, m)
        for oh, dd in ((OH1, D1), (OH2, D2)):
            tt(V, T64, oh, E64, ALU.mult, V.mark(), mk)
            reduce(dd, T64, ALU.add, V.mark())
        copy(V, IT[:, 512:576], STR, V.mark())
        reduce(sc[:, 60:61], CNT, ALU.max, V.mark())
        mints = copy(V, IT[:, 576:577], sc[:, 60:61], V.mark())
        for c in range(4):
            ts(V, PM[:, c, :], IO, D1[:, c:c + 1], None, ALU.is_equal, None, V.mark(), mio)
            mpm = stt(PM[:, c, :], IO, D2[:, c:c + 1], PM[:, c, :], ALU.is_equal, ALU.add, V.mark())
        for dt_ in range(8):
            for q in range(2):
                b = bank()
                for c in range(4):
                    m = mm(b.ap[:, :], HT[:, c, dt_ * 128:dt_ * 128 + 128], PM[:, c, q * 512:q * 512 + 512],
                           c == 0, c == 3, c == 3, hts, mpm)
                b.free = copy(S if q else V, XSO[:, dt_, q * 512:q * 512 + 512], b.ap[:, :], m)
        G.do(lambda e: e.memset(XSO[:, :, 1024:1536], 0.0))
        join()
        if stop == "route":
            taps.update({"XSO": XSO, "LG": LG, "OH1": OH1, "OH2": OH2, "D1": D1, "D2": D2, "W1": W1, "W2": W2, "STR": STR, "CNT": CNT})
            return finish(nc, locals())
        table(SET_SILU)
        o = n0
        XWR = Ring([Slot(A[:, o + 1024 * i:o + 1024 * i + 1024].rearrange("p (k n) -> p k n", n=128)) for i in range(2)])
        SIL, HID, HDT = (Ring([Slot(A[:, o + c + 256 * i:o + c + 256 * i + 256]) for i in range(2)])
                         for c in (2048, 2560, 3072))
        top[0] -= 576
        OUT = Ring([Slot(small), Slot(alloc(1024))])
        wge, wue, wde = d["w_gate_e"][0], d["w_up_e"][0], d["w_down_e"][0]

        def window(q, e_, use):
            def f(e):
                v = e.value_load(IT[0:1, 512 + e_:513 + e_], min_val=0, max_val=1024)
                return use(e, v)
            return f

        def gate_up(e_, k0):
            s = WX.next()
            dst = s.ap.rearrange("p (k c) -> p k c", c=512)
            for i, w in enumerate((wge, wue)):
                s.n += 16
                m = dma(dst[:, :, 256 * i:256 * i + 256],
                        w[e_][k0 * 128:k0 * 128 + 512, :].rearrange("(k p) c -> p k c", p=128), s.sem, s.n, s.free)
            return dst, m, s

        def experts():
            u = {}

            def e0(i):
                t = u[i] = {}
                x = XWR.next()
                for j in range(2):
                    mx = V.do(window(V, 2 * i + j, lambda e, v, j=j: e.tensor_copy(
                        x.ap[:, :, 64 * j:64 * j + 64], XSO[:, :, bass.ds(v, 64)])), x.free)
                t["b"] = b = bank()
                for k0 in (0, 4):
                    ws = [gate_up(2 * i + j, k0) for j in range(2)]
                    for k in range(4):
                        for j, (w, m, s) in enumerate(ws):
                            mk = mm(b.ap[64 * j:64 * j + 64, :], x.ap[:, k0 + k, 64 * j:64 * j + 64], w[:, k, :],
                                    k0 + k == 0, k0 + k == 7, k == 3, m, mx)
                    for w, m, s in ws:
                        s.free = mk
                x.free = mk
                sl, hd = SIL.next(), HID.next()
                m = act(sl.ap, b.ap[:, 0:256], ACT.Silu, mk, sl.free)
                m = b.free = sl.free = tt(V, hd.ap, sl.ap, b.ap[:, 256:512], ALU.mult, m, hd.free)
                t.update(hd=hd, m=m)

            def e1(i):
                t = u[i]
                wd = [wload(wde[2 * i + j], 0, 2, 0, 1024, WX) for j in range(2)]
                b = bank(XR)
                for f in range(2):
                    mk = tr(b.ap[:, f * 128:f * 128 + 128], t["hd"].ap[:, f * 128:f * 128 + 128], f == 1, t["m"])
                t["hd"].free = mk
                ht = HDT.next()
                b.free = m = copy(V, ht.ap, b.ap[:, 0:256], mk, ht.free)
                t["o"] = o = OUT.next()
                bs = [bank(), bank()]
                for q, b in enumerate(bs):
                    for f in range(2):
                        for j, (w, mw, s) in enumerate(wd):
                            mk = mm(b.ap[64 * j:64 * j + 64, :], ht.ap[:, f * 128 + 64 * j:f * 128 + 64 * j + 64],
                                    w[:, f, q * 512:q * 512 + 512], f == 0, f == 1, f == 1, m, mw)
                    b.free = copy(S if q else V, o.ap[:, q * 512:q * 512 + 512], b.ap[:, :], mk, o.free)
                    t["mo", q] = b.free
                ht.free = mk
                for w, mw, s in wd:
                    s.free = mk

            def e2(i):
                t = u.pop(i)
                for q in range(2):
                    b = bank(XR)
                    for j in range(4):
                        f = q * 4 + j
                        mk = tr(b.ap[:, j * 128:j * 128 + 128], t["o"].ap[:, f * 128:f * 128 + 128], j == 3, t["mo", q])
                    bv = b.ap[:, :].rearrange("p (a n) -> p a n", n=128)
                    for j in range(2):
                        b.free = S.do(window(S, 2 * i + j, lambda e, v, j=j, q=q, bv=bv: e.activation(
                            YSO[:, 4 * q:4 * q + 4, bass.ds(v, 64)], bv[:, :, 64 * j:64 * j + 64], ACT.Copy)),
                            mk, S.mark())
                t["o"].free = mk

            yield from staged([e0, e1, e2], 32, (0, 1, 2), True)

        run_all(experts())
        join()
        fallback(nc, locals())
        if stop == "moe":
            taps.update({"YSO": YSO})
            return finish(nc, locals())

        top[0] = base + 3 * 2048
        YK = tiles(8, 1024)
        assert top[0] <= base + 3 * 2048 + 12288
        IOT = A[:, n0:n0 + 1024]
        mio = dma(IOT, d["iota1024"], s_x, 64, everything())
        PWF = tiles(4, 1024)
        PWG = [A[:, base + 1024 * i:base + 1024 * i + 1024] for i in range(4)]
        for c in range(4):
            pv = PWF[:, c, :]
            m = ts(V, pv, IOT, D1[:, c:c + 1], W1[:, c:c + 1], ALU.is_equal, ALU.mult, mio)
            m2 = ts(V, PWG[c], IOT, D2[:, c:c + 1], W2[:, c:c + 1], ALU.is_equal, ALU.mult, mio)
            mpf = tt(G, pv, pv, PWG[c], ALU.add, m, m2)
        for s_ in range(8):
            for q in range(2):
                b = bank(XR)
                for j in range(4):
                    m = tr(b.ap[:, j * 128:j * 128 + 128], YSO[:, q * 4 + j, s_ * 128:s_ * 128 + 128], j == 3)
                b.free = copy(S, YK[:, s_, q * 512:q * 512 + 512], b.ap[:, :], m)
        yk = S.mark()
        join()
        PWA = YSO.rearrange("p a b -> p (a b)")[:, 0:4096].rearrange("p (s t) -> p s t", t=512)
        for s_ in range(8):
            b = bank(XR)
            for c in range(4):
                mk = tr(b.ap[:, c * 128:c * 128 + 128], PWF[:, c, s_ * 128:s_ * 128 + 128], c == 3, mpf)
            b.free = copy(S if s_ % 2 else V, PWA[:, s_, :], b.ap[:, :], mk)
        mpw = [S.mark(), V.mark()]
        for dt_ in range(8):
            b = bank()
            for s_ in range(8):
                mk = mm(b.ap[:, :], YK[:, s_, dt_ * 128:dt_ * 128 + 128], PWA[:, s_, :], s_ == 0, s_ == 7, s_ == 7,
                        mpw, yk)
            r = R[:, dt_, 16:T2]
            b.free = tt(V, r, r, b.ap[:, :], ALU.add, mk)
        mR = V.mark()
        join()
        if stop == "x2":
            taps.update({"R": R[:, :, 16:T2]})
            return finish(nc, locals())
        second(nc, locals())
        finish(nc, locals())


def second(nc, L):
    import math
    g = dict(L)
    C, R, PE, V, S, G, d, ctx = (g[k] for k in ("C", "R", "PE", "V", "S", "G", "d", "ctx"))
    join, dma, act, tt, ts, stt, copy, reduce, mm, tr, bank, BR, XR = (
        g[k] for k in ("join", "dma", "act", "tt", "ts", "stt", "copy",
                       "reduce", "mm", "tr", "bank", "BR", "XR"))
    later, table, head_norm_rope = (g[k] for k in ("later", "table", "head_norm_rope"))
    s_x, s_out, SP, bc, bmid, everything = (g[k] for k in ("s_x", "s_out", "SP", "bc", "bmid", "everything"))
    table(SET_EXP_LN)
    g["early"].close()

    class Part:

        def __init__(self, stack, name, n, dt=F32):
            self.t, self.n, self.at = stack.enter_context(nc.sbuf_tensor(name, [128, n], dt)), n, 0

        def take(self, n):
            self.at += n
            assert self.at <= self.n, (self.at, self.n)
            return self.t[:, self.at - n:self.at]

        def tiles(self, k, n):
            return self.take(k * n).rearrange("p (k n) -> p k n", n=n)

        def ring(self, k, n):
            return Ring([Slot(self.take(n)) for _ in range(k)])

    KEEP = Part(ctx, "keep", 5 * 1024 + 2 * T2)
    SPLIT = Part(ctx, "split", 16 * T2 + 3 * 2048, F32R)
    WR = Ring([Slot(KEEP.take(1024), sem_) for sem_ in g["slot_sems"][0:5]])
    for s in WR.slots:
        s.free = everything()
    counts = {id(s.sem): s.n for s in list(g["WX"].slots) + list(g["WR"].slots)}
    for s in WR.slots:
        s.n = counts[id(s.sem)]
    WS = SPLIT.ring(3, 2048)
    CS2 = KEEP.take(2 * T2)
    COS, SIN = CS2[:, 0:T2], CS2[:, T2:2 * T2]
    HH, HL = SPLIT.tiles(8, T2), SPLIT.tiles(8, T2)
    cs = [128 * i for i in range(8)]

    def whole(ap):
        return ap.bitcast(F32)

    def cut(x, hi, lo, mark, *free, by=G):
        m = act(hi, x, ACT.Copy, mark, *free)
        return [m, tt(by, lo, x, whole(hi), ALU.subtract, m)]

    wq, wkv, wqb, wao, wbo = (d["a_w_qkv_2"][0], d["kv_w_2"], d["b_w_q_2"][0], d["a_w_o_2"][0], d["b_w_o_2"][0])
    wmi, wmo = ([d[n][i] for i in range(2)] for n in ("mlp_w_in_2", "mlp_w_out_2"))
    plan = []

    for p in range(4):
        plan += [(wq, 0, 8, o + 256 * p + x, 128, None) for o in (0, 1024) for x in (0, 128)]
        plan += [(wq, k0, 4, 2048 + 256 * p, 256, None) for k0 in (0, 4)]
    plan += [(wao, 0, 8, c, 128, None) for c in cs]

    def mlp_plan(n):
        ins = [[(wmi[n], 0, 8, 1024 * q + c, 128, None) for c in cs] for q in range(4)]
        outs = [[(wmo[n], 8 * q, 8, c, 128, None) for c in cs] for q in range(4)]
        return ins[0] + ins[1] + outs[0] + ins[2] + outs[1] + ins[3] + outs[2] + outs[3]

    by_v = len(plan)
    plan += mlp_plan(0)
    for p in range(4):
        plan += [(wkv, 0, 8, 256 * p + x, 128, C["kvg"]) for x in (0, 128)]
        plan += [(wqb, 0, 8, 256 * p + x, 128, C["bng"]) for x in (0, 128)]
        plan += [(wkv, k0, 4, 1024 + 256 * p, 256, C["kvg"]) for k0 in (0, 4)]
    plan += [(wbo, 0, 8, c, 128, None) for c in cs]
    plan += mlp_plan(1)
    made = []

    def make():
        view, k0, nk, c0, nc_, gain = plan[len(made)]
        s, w = WR.next(), WS.next()
        s.n += 16
        v3 = lambda a: a.rearrange("p (k c) -> p k c", c=nc_)
        x, hi, lo = v3(s.ap), v3(w.ap[:, 0:1024]), v3(w.ap[:, 1024:2048])
        m = dma(x, view[k0 * 128:(k0 + nk) * 128, c0:c0 + nc_].rearrange("(k p) c -> p k c", p=128), s.sem, s.n, s.free)
        if gain is None:
            m = cut(x, hi, lo, m, w.free, by=V if len(made) < by_v else G)
        else:
            for k in range(nk):
                gk = gain[:, k0 + k:k0 + k + 1]
                m1 = act(hi[:, k, :], x[:, k, :], ACT.Copy, m, w.free, scale=gk)
            m = [m1, stt_k(lo, x, gain[:, k0:k0 + nk], hi, m1)]
        s.free = m
        made.append((view, k0, c0, hi, lo, m, w))

    def stt_k(lo, x, gains, hi, mark):
        for k in range(lo.shape[1]):
            m = stt(lo[:, k, :], x[:, k, :], gains[:, k:k + 1], whole(hi[:, k, :]), ALU.mult, ALU.subtract, mark)
        return m

    used = [0]

    def weights(view, k0, c0):
        while len(made) < min(used[0] + 2, len(plan)):
            make()
        w = made[used[0]]
        used[0] += 1
        assert w[0] is view and w[1:3] == (k0, c0)
        return w[3:]

    def product(b, l, r, first, last, mark, *marks):
        mm(b, l[0], r[0], first, False, False, *marks)
        mm(b, l[0], r[1], False, False, False)
        return mm(b, l[1], r[0], False, last, mark)

    def linear(view, cols, X, ready, splits, evac, k0=0):
        for i, c in enumerate(cols):
            hi, lo, m, s = weights(view, k0, c)
            banks = [bank() for _ in splits]
            for k in range(8):
                for b, (n0, n1) in zip(banks, splits):
                    mark = product(b.ap[:, 0:n1 - n0], (hi[:, k, :], lo[:, k, :]), [x[:, k, n0:n1] for x in X],
                                   k == 0, k == 7, k == 7 and (n0, n1) == splits[-1], m, ready[k])
            s.free = mark
            evac(i, banks, mark)
            later.tick()
            yield

    def linear_v(view, c0, X, ready, evac):
        ws = [weights(view, 0, c0), weights(view, 4, c0)]
        for ti, (t0, t1) in enumerate(TILES2):
            b = bank()
            for k in range(8):
                hi, lo, m, s = ws[k // 4]
                mark = product(b.ap[0:t1 - t0, 0:256], [x[:, k, t0:t1] for x in X], (hi[:, k % 4, :], lo[:, k % 4, :]),
                               k == 0, k == 7, k == 7, m, ready[k])
            evac(ti, c0, c0 + 256, b, mark)
            if ti == 4:
                for w in ws:
                    w[3].free = mark
            later.tick()
            yield

    def norm(gains, splits, ready, sq, rs, xs):
        done = [[] for _ in range(8)]
        ts_ = []
        for n0, n1 in splits:
            b = bank()
            n = n1 - n0
            for k in range(8):
                s = sq.next()
                if k % 2:
                    m = act(s.ap[:, 0:n], R[:, k, n0:n1], ACT.Square, ready, s.free)
                else:
                    m = tt(V, s.ap[:, 0:n], R[:, k, n0:n1], R[:, k, n0:n1], ALU.mult, ready, s.free)
                s.free = m = mm(b.ap[:, 0:n], C["ones"], s.ap[:, 0:n], k == 0, k == 7, True, m)
            t = rs.next()
            b.free = act(t.ap[:, 0:n], b.ap[:, 0:n], ACT.Ln, m, t.free, bias=C["eps"], scale=1.0 / 1024)
            ts_.append((t, act(t.ap[:, 0:n], t.ap[:, 0:n], ACT.Exp, b.free, scale=-0.5)))
        for k in range(8):
            for (n0, n1), (t, m) in zip(splits, ts_):
                n = n1 - n0
                x = xs.next()
                if gains is None:
                    t.free = m1 = tt(V, x.ap[:, 0:n], R[:, k, n0:n1], t.ap[:, 0:n], ALU.mult, m, x.free)
                else:
                    t.free = m1 = stt(x.ap[:, 0:n], R[:, k, n0:n1], gains[:, k:k + 1], t.ap[:, 0:n],
                                      ALU.mult, ALU.mult, m, x.free)
                x.free = c = cut(x.ap[:, 0:n], HH[:, k, n0:n1], HL[:, k, n0:n1], m1)
                done[k] += c
        return done

    stack = ExitStack()
    P = Part(stack, "attention", 16 * T2 + 8 * T2 + 5 * 1024 + 8 * 512)
    QT, KT, OT = P.tiles(8, T2), P.tiles(8, T2), P.tiles(8, T2)
    VT = P.tiles(5, 1024)
    o = P.at
    SQ, RS, XB = P.ring(2, 264), P.ring(2, 264), P.ring(3, 264)
    MT = P.take(1024)
    dma(CS2, d["cs2"], s_x, 80, everything())
    mmt = dma(MT[0:16, :], d["meta_tokens_2"], s_x, 96)
    b = bank()
    for k in range(8):
        m = tr(b.ap[:, k * 16:k * 16 + 16], MT[0:16, k * 128:k * 128 + 128], k == 7, mmt)
    b.free = m = copy(V, R[:, :, 0:16], b.ap[:, 0:128].rearrange("p (k n) -> p k n", n=16), m)
    h = norm(C["ang"], HALVES2, m, SQ, RS, XB)
    H = (HH, HL)

    def evac_to(O, scale):
        def f(i, banks, mark):
            for b, (n0, n1), q in zip(banks, HALVES2, (S, V)):
                if q is S:
                    b.free = act(O[:, i, n0:n1], b.ap[:, 0:n1 - n0], ACT.Copy, mark, scale=scale)
                else:
                    b.free = ts(V, O[:, i, n0:n1], b.ap[:, 0:n1 - n0], scale, None, ALU.mult, None, mark)
        return f

    def evac_v(ti, a, b_, b, mark):
        n = TILES2[ti][1] - TILES2[ti][0]
        o = a % 1024
        b.free = copy(S if ti % 2 else V, VT[0:n, ti, o:o + b_ - a], b.ap[0:n, 0:b_ - a], mark)

    join()
    P.at = o
    EB, WB = P.ring(4, 512), P.ring(4, 512)
    qkv = {}

    def projections(p):
        c = [256 * p, 256 * p + 128]
        off = lambda f, o: (lambda i, banks, mark: f(i + o, banks, mark))
        yield from linear(wq, c, H, h, HALVES2, off(evac_to(QT, 0.125), 2 * p))
        yield from linear(wq, [1024 + x for x in c], H, h, HALVES2, off(evac_to(KT, 1.0), 2 * p))
        yield from linear_v(wq, 2048 + c[0], H, h, evac_v)
        qkv[p] = [S.mark(), V.mark()]

    def ksize(k):
        return TILES2[k][1] - TILES2[k][0]

    def areas(i, tq):
        return [(128, 0, (i + 1) * tq)] if i < 4 else [(128, 0, 4 * tq), (16, 4 * tq, 5 * tq)]

    units = []
    for p in range(4):
        units += [([hp], i, par) for hp in (2 * p, 2 * p + 1) for i in range(4) for par in range(2)]
        units += [([2 * p, 2 * p + 1], 4, par) for par in range(2)]
    u = {}

    def b0(n):
        hps, i, par = units[n]
        t = u[n] = {}
        w, tq = ksize(i), ksize(i) * len(hps)
        pr = slice(par * 64, par * 64 + 64)
        t["b"] = b = bank(XR)
        for k in range(i + 1):
            for x, hp in enumerate(hps):
                m = mm(b.ap[0:ksize(k), k * tq + x * w:k * tq + x * w + w], KT[pr, hp, TILES2[k][0]:TILES2[k][1]],
                       QT[pr, hp, TILES2[i][0]:TILES2[i][1]], k == 0 and x == 0, False, k == i and hp == hps[-1],
                       qkv[hp // 2])
        t["e"] = e = EB.next()
        for r, a, z in areas(i, tq):
            x = e.ap[0:r, a:z]
            y = b.ap[0:r, a:z]
            m1 = ts(V, x, y, 40.0, None, ALU.min, None, m, e.free)
            m1 = act(x, x, ACT.Exp, m1)
            m1 = act(x, x, ACT.Ln, m1, bias=C["one"][0:r, :])
            t["ms"] = tt(V, x, x, y, ALU.max, m1)
        t["md"] = causal(e.ap, i, w, tq, t["ms"])

    def causal(e, i, w, tq, mark):
        x = e[0:w, i * tq:i * tq + tq]
        pattern = [[1, w]]
        if tq > w:
            x, pattern = x.rearrange("p (a n) -> p a n", n=w), [[0, tq // w], [1, w]]
        return G.do(lambda q: q.affine_select(out=x, in_=x, compare_op=ALU.is_gt, fill=0.0, base=0,
                                              pattern=pattern, channel_multiplier=-1), mark)

    def b1(n):
        hps, i, par = units[n]
        t = u[n]
        w_, tq = ksize(i), ksize(i) * len(hps)
        b, e = t["b"], t["e"]
        for j in range(i + 1):
            r = ksize(j)
            c = slice(j * tq, j * tq + tq)
            if j > 0:
                mm(b.ap[:, 0:j * tq].rearrange("p (k n) -> p k n", n=tq), C["negones"][0:r, :],
                   bmid(e.ap[0:r, c], j), False, False, False, t["ms"], t["md"])
            m = mm(b.ap[0:r, c], C["negfrom"][0:r, 0:r], e.ap[0:r, c], False, j == i, j == i, t["ms"], t["md"])
        e.free = m
        t["w"] = w = WB.next()
        for r, a, z in areas(i, tq):
            m1 = b.free = act(w.ap[0:r, a:z], b.ap[0:r, a:z], ACT.Exp, m, w.free)
        t["mw"] = causal(w.ap, i, w_, tq, m1)

    def b2(n):
        hps, i, par = units[n]
        if par == 0:
            return
        w, tq = ksize(i), ksize(i) * len(hps)
        b = bank(XR)
        for par in range(2):
            t = u.pop(n - 1 + par)
            for x, hp in enumerate(hps):
                for k in range(i + 1):
                    r = ksize(k)
                    m = mm(b.ap[par * 64:par * 64 + 64, x * w:x * w + w],
                           VT[0:r, k, (2 * hp + par) * 64:(2 * hp + par) * 64 + 64],
                           t["w"].ap[0:r, k * tq + x * w:k * tq + x * w + w], k == 0, k == i, k == i, t["mw"])
            t["w"].free = m
        b.free = copy(V if i % 2 else S, OT[:, hps[0]:hps[-1] + 1, TILES2[i][0]:TILES2[i][1]],
                      b.ap[:, 0:tq].rearrange("p (a n) -> p a n", n=w), m)

    run_all(projections(0))
    att = staged([b0, b1, b2], 72, (0, 2, 3), True)
    for p in range(4):
        nxt = projections(p + 1) if p < 3 else iter(())
        for n in range(18):
            next(att)
            if n % 2:
                next(nxt, None)
        run_all(nxt)
    run_all(att)

    m = [V.mark(), S.mark(), PE.mark()]
    ot = [cut(OT[:, k, :], HH[:, k, :], HL[:, k, :], m, by=V if k % 2 else G) for k in range(8)]

    def evac_res(splits):
        def f(i, banks, mark):
            for b, (n0, n1) in zip(banks, splits):
                r = R[:, i, n0:n1]
                b.free = tt(V, r, r, b.ap[:, 0:n1 - n0], ALU.add, mark)
        return f

    run_all(linear(wao, cs, H, ot, HALVES2, evac_res(HALVES2)))

    def mlp(n, splits):
        with ExitStack() as mine:
            F = Part(mine, f"hidden{n}", 32 * T2, F32R)
            P = Part(mine, f"mlp{n}", 4 * 512 + 5 * 512)
            HID = [(F.tiles(8, T2), F.tiles(8, T2)) for _ in range(2)]
            SQ, RS, XB = P.ring(2, 512), P.ring(2, 512), P.ring(5, 512)
            h = norm(C["mg"][:, 8 * n:8 * n + 8], splits, V.mark(), SQ, RS, XB)
            hid = {}

            def into(q):
                hi, lo = HID[q % 2]
                hid[q] = []

                def evac(i, banks, mark):
                    ms = []
                    for b, (n0, n1) in zip(banks, splits):
                        x = XB.next()
                        xa = x.ap[:, 0:n1 - n0]
                        m = act(xa, b.ap[:, 0:n1 - n0], ACT.Relu, mark, x.free)
                        m = b.free = tt(V, xa, xa, b.ap[:, 0:n1 - n0], ALU.mult, m)
                        x.free = cut(xa, hi[:, i, n0:n1], lo[:, i, n0:n1], m)
                        ms += x.free
                    hid[q].append(ms)

                run_all(linear(wmi[n], [1024 * q + c for c in cs], H, h, splits, evac))

            def out_of(q):
                run_all(linear(wmo[n], cs, HID[q % 2], hid[q], splits, evac_res(splits), k0=8 * q))

            into(0)
            into(1)
            out_of(0)
            into(2)
            out_of(1)
            into(3)
            out_of(2)
            out_of(3)
            join()

    join()
    stack.close()
    if g["stop"] == "a1":
        g["taps"].update({"R": R, "OT": OT})
        return
    mlp(0, HALVES2)
    if g["stop"] == "a2":
        g["taps"].update({"R": R})
        return

    stack = ExitStack()
    P = Part(stack, "attention2", 16 * T2 + 8 * T2 + 5 * 1024 + 12 * 264 + 3 * 2 * T2 + 1280 + 24 + 16)
    QT, KT, OT = P.tiles(8, T2), P.tiles(8, T2), P.tiles(8, T2)
    VT = P.tiles(5, 1024)
    HB = P.ring(12, 264)
    sm = P.take(16)
    col = lambda i: sm[:, i:i + 1]
    lam_init = 0.8 - 0.6 * math.exp(-0.3)
    o = P.at
    LB = P.take(128)
    lam4 = C["lam"].rearrange("p (a b n) -> p a b n", a=2, b=2)
    m = tt(V, LB.rearrange("p (a n) -> p a n", a=2), lam4[:, :, 0, :], lam4[:, :, 1, :], ALU.mult)
    m = reduce(sm[:, 0:2], LB.rearrange("p (a n) -> p a n", a=2), ALU.add, m)
    m = act(sm[:, 0:2], sm[:, 0:2], ACT.Exp, m)
    m = tt(V, col(2), col(1), col(0), ALU.subtract, m)
    NLAM = col(2)
    m = ts(V, NLAM, NLAM, -lam_init, None, ALU.add, None, m)
    m = mlam = ts(V, col(3), C["subg"], 1.0 - lam_init, None, ALU.mult, None, m)
    SQ, RS, XB = P.ring(2, 512), P.ring(2, 512), P.ring(3, 264)
    h = norm(None, HALVES2, V.mark(), SQ, RS, XB)

    def evac_nr(gain, O, o, splits):
        def f(i, banks, mark):
            for b, (n0, n1) in zip(banks, splits):
                head_norm_rope(b, n1 - n0, gain, COS[:, n0:n1], SIN[:, n0:n1], O[:, i + o, n0:n1], HB, mark)
        return f

    kvq = {}

    def projections2(p):
        c = [256 * p, 256 * p + 128]
        yield from linear(wkv, c, H, h, HALVES2, evac_nr(C["kkg"], KT, 2 * p, HALVES2))
        yield from linear(wqb, c, H, h, HALVES2, evac_nr(C["qqg"], QT, 2 * p, HALVES2))
        yield from linear_v(wkv, 1024 + c[0], H, h, evac_v)
        kvq[p] = [S.mark(), V.mark()]

    run_all(projections2(0))
    later.flush()
    kvq[0] = [S.mark(), V.mark()]
    join()
    P.at = o
    SB, WT = P.ring(3, 2 * T2), P.ring(2, 640)
    VEC = P.ring(3, 8)
    un = [(hh, i) for hh in range(8) for i in range(4)]
    w_ = {}

    def c0(n):
        hh, i = un[n]
        t = w_[n] = {}
        q0, kl = 16 + 128 * i, 144 + 128 * i
        t["s"] = s = SB.next()
        sv = s.ap.rearrange("p (a n) -> p a n", a=2)
        for a in range(2):
            pr = slice(a * 64, a * 64 + 64)
            for k0, k1 in [(0, kl)] if i < 3 else HALVES2:
                b = bank(XR)
                m = mm(b.ap[:, 0:k1 - k0], QT[pr, hh, q0:q0 + 128], KT[pr, hh, k0:k1], True, True, True, kvq[hh // 2])
                if a == 0:
                    ma = b.free = act(sv[:, a, k0:k1], b.ap[:, 0:k1 - k0], ACT.Copy, m, s.free, scale=0.125)
                else:
                    mb = b.free = ts(V, sv[:, a, k0:k1], b.ap[:, 0:k1 - k0], 0.125, None, ALU.mult, None, m, s.free)
        dg = sv[:, :, kl - 128:kl]
        m = tt(V, dg, dg, bmid(C["amask"][:, 128:256], 2), ALU.add, ma, mb)
        t["v"] = v = VEC.next()
        m = reduce(v.ap[:, 0:2], sv[:, :, 0:kl], ALU.max, m, v.free)
        m = ts(V, v.ap[:, 2:4], v.ap[:, 0:2], -1.0, None, ALU.mult, None, m)
        for a in range(2):
            x = sv[:, a, 0:kl]
            m2 = act(x, x, ACT.Exp, m, bias=v.ap[:, 2 + a:3 + a], accum_out=v.ap[:, 4 + a:5 + a])
        m = V.do(lambda e: e.reciprocal(v.ap[:, 4:6], v.ap[:, 4:6]), m2)
        m = tt(V, v.ap[:, 5:6], v.ap[:, 5:6], NLAM, ALU.mult, m)
        m = ts(V, sv[:, 0, 0:kl], sv[:, 0, 0:kl], v.ap[:, 4:5], None, ALU.mult, None, m)
        t["m"] = v.free = stt(sv[:, 0, 0:kl], sv[:, 1, 0:kl], v.ap[:, 5:6], sv[:, 0, 0:kl], ALU.mult, ALU.add, m)

    def c1(n):
        hh, i = un[n]
        t = w_[n]
        t["w"] = w = WT.next()
        t["mw"] = []
        last = i + 1
        for ks in [range(i + 2)] if i < 3 else [range(4), [4]]:
            b = bank(XR)
            for k in ks:
                n_ = 16 if k == last else 128
                c = (k - ks[0]) * 128
                m = tr(b.ap[0:n_, c:c + 128], t["s"].ap[:, k * 128:k * 128 + n_], k == ks[-1], t["m"])
            t["s"].free = m
            full = len([k for k in ks if k < last]) * 128
            if full:
                b.free = copy(S, w.ap[:, 0:full], b.ap[:, 0:full], m, w.free)
                t["mw"].append(b.free)
            if ks[-1] == last:
                b.free = copy(S, w.ap[0:16, last * 128:last * 128 + 128], b.ap[0:16, full:full + 128], m, w.free)
                t["mw"].append(b.free)

    def c2(n):
        hh, i = un[n]
        t = w_.pop(n)
        b = bank()
        for k in range(i + 2):
            r = 16 if k == i + 1 else 128
            m = mm(b.ap[:, 0:128], VT[0:r, k, hh * 128:hh * 128 + 128], t["w"].ap[0:r, k * 128:k * 128 + 128],
                   k == 0, k == i + 1, k == i + 1, t["mw"])
        t["w"].free = m
        b.free = t["mo"] = copy(V, OT[:, hh, 16 + 128 * i:144 + 128 * i], b.ap[:, 0:128], m)

    def c3(n):
        hh, i = un[n]
        if i < 3:
            return
        o, s = OT[:, hh, 16:T2], SB.next()
        x, y = s.ap[:, 0:512], s.ap[:, T2:T2 + 512]
        m = act(x, o, ACT.Square, V.mark(), s.free)
        b = bank()
        m = mm(b.ap[:, :], C["ones"], x, True, True, True, m)
        b.free = m = act(y, b.ap[:, :], ACT.Ln, m, bias=C["eps"], scale=1.0 / 128)
        m = act(y, y, ACT.Exp, m, scale=-0.5)
        s.free = stt(o, o, col(3), y, ALU.mult, ALU.mult, m, mlam)

    att = staged([c0, c1, c2, c3], 32, (0, 2, 3, 4), True)
    for p in range(4):
        nxt = projections2(p + 1) if p < 3 else iter(())
        for n in range(8):
            next(att)
            next(nxt, None)
        run_all(nxt)
        later.flush()
        kvq[p + 1] = [S.mark(), V.mark()]
    run_all(att)
    LAST = [(16, T2)]
    m0 = [V.mark(), PE.mark()]
    ot = [cut(OT[:, k, 16:T2], HH[:, k, 16:T2], HL[:, k, 16:T2], m0) for k in range(8)]
    run_all(linear(wbo, cs, H, ot, LAST, evac_res(LAST)))
    if g["stop"] == "b1":
        g["taps"].update({"R": R, "OT": OT})
        return
    join()
    stack.close()
    mlp(1, LAST)

    OB = Part(ctx, "result", 4096).tiles(4, 1024)
    n = 0
    for c in range(4):
        for q in range(2):
            b = bank()
            for j in range(4):
                m = tr(b.ap[:, j * 128:j * 128 + 128], R[:, q * 4 + j, 16 + c * 128:144 + c * 128], j == 3)
            b.free = copy(S if q else V, OB[:, c, q * 512:q * 512 + 512], b.ap[:, :], m)
        n += 16
        dma(g["out"][0, c * 128:c * 128 + 128, :], OB[:, c, :], s_out, n, S.mark(), V.mark())
    SP.wait((s_out, n))


def fallback(nc, L):
    A, IT, PB, XSO, YSO, XW, W0, d = (L[k] for k in ("A", "IT", "PB", "XSO", "YSO", "XW", "W0", "d"))
    PE, V, S, SP, sem = (L[k] for k in ("PE", "V", "S", "SP", "sem"))
    f_w, f_x, f_p, f_g, f_h, f_d, f_y = (sem(f"f_{n}") for n in "wxpghdy")
    go = {n: sem(f"go_{n}") for n in ("pe", "dve", "act")}
    wg = W0[:, 0:2048].rearrange("p (k c) -> p k c", k=8)
    wu = W0[:, 2048:4096].rearrange("p (k c) -> p k c", k=8)
    wd = W0[:, 4096:6144].rearrange("p (k c) -> p k c", k=2)
    sil = W0[:, 6144:7168].rearrange("p (a n) -> p a n", a=2)
    hid = W0[:, 7168:8192].rearrange("p (a n) -> p a n", a=2)

    def many(e):
        return e.value_load(IT[0:1, 576:577], min_val=0, max_val=512) > 64

    def begin(e, name):
        e.wait_ge(go[name], 1)
        e.sem_clear(go[name])

    def start(e, i):
        return e.value_load(IT[0:1, bass.ds(512 + i, 1)], min_val=0, max_val=1024)

    def sp(e):
        with e.If(many(e)):
            with e.Fori(0, 64) as i:
                for dst, name, k in ((wg, "w_gate_e", 8), (wu, "w_up_e", 8), (wd, "w_down_e", 2)):
                    src = d[name][0][bass.ds(i, 1)].rearrange("a (k p) c -> p (a k) c", p=128)
                    e.dma_start(dst, src).then_inc(f_w, 16)
                for n in go:
                    e.sem_inc(go[n], 1)
                e.wait_ge(f_y, 8)
                for s in (f_w, f_x, f_p, f_g, f_h, f_d, f_y):
                    e.sem_clear(s)
            for n in go:
                e.sem_inc(go[n], 1)

    def pe(e):
        with e.If(many(e)):
            with e.Fori(0, 64) as i:
                begin(e, "pe")
                e.wait_ge(f_w, 48)
                e.wait_ge(f_x, 1)
                for n, w in enumerate((wg, wu)):
                    for f in range(2):
                        for k in range(8):
                            m = e.matmul(PB[2 * n + f][:, :], w[:, k, f * 128:f * 128 + 128], XW[:, k, :],
                                         start=k == 0, stop=k == 7)
                m.then_inc(f_p, 1)
                e.wait_ge(f_h, 1)
                for t in range(8):
                    for f in range(2):
                        m = e.matmul(PB[(t + 4) % 8][:, :], wd[:, f, t * 128:t * 128 + 128], hid[:, f, :],
                                     start=f == 0, stop=f == 1)
                m.then_inc(f_d, 1)
            begin(e, "pe")

    def dve(e):
        with e.If(many(e)):
            with e.Fori(0, 64) as i:
                begin(e, "dve")
                e.tensor_copy(XW, XSO[:, :, bass.ds(start(e, i), 512)]).then_inc(f_x, 1)
                e.wait_ge(f_g, 2)
                e.tensor_tensor(hid[:, 0, :], sil[:, 0, :], PB[2][:, :], ALU.mult)
                e.tensor_tensor(hid[:, 1, :], sil[:, 1, :], PB[3][:, :], ALU.mult).then_inc(f_h, 1)
            begin(e, "dve")

    def act(e):
        with e.If(many(e)):
            with e.Fori(0, 64) as i:
                begin(e, "act")
                e.wait_ge(f_p, 1)
                for f in range(2):
                    e.activation(sil[:, f, :], PB[f][:, :], ACT.Silu).then_inc(f_g, 1)
                e.wait_ge(f_d, 1)
                v = start(e, i)
                for t in range(8):
                    e.activation(YSO[:, t, bass.ds(v, 512)], PB[(t + 4) % 8][:, :], ACT.Copy).then_inc(f_y, 1)
            begin(e, "act")

    SP.plain(sp, L["everything"]())
    PE.plain(pe)
    V.plain(dve)
    S.plain(act)


def finish(nc, L):
    taps, S, SP, join, stop = L["taps"], L["S"], L["SP"], L["join"], L["stop"]
    if stop:
        join()
        SP.wait(L["everything"]())
        s_out = L["s_out"]
        n = 0
        for name, ap in taps.items():
            shape = list(ap.shape)
            t = nc.dram_tensor("tap_" + name, shape, ap.dtype, kind="ExternalOutput").ap()
            n += 16
            SP.items.append(lambda e, t=t, ap=ap: e.dma_start(t, ap).then_inc(s_out, 16))
        SP.items.append(lambda e: e.wait_ge(s_out, n))
    block = L["ctx"].enter_context(nc.Block())
    block.sync(lambda e: L["SP"].emit(e))
    block.tensor(lambda e: L["PE"].emit(e))
    block.vector(lambda e: L["V"].emit(e))
    block.scalar(lambda e: L["S"].emit(e))
    block.gpsimd(lambda e: L["G"].emit(e))


def host_arrays(i):
    cp, c2 = const_parts(), const2_parts()
    a = {
        "x": i["x"],
        "pos": np.ascontiguousarray(np.broadcast_to(i["positions"].reshape(1, -1), (128, 512))),
        "consts": np.concatenate(list(cp.values()), 1),
        "smalls": small_array(i),
        "iota1024": c2["iota1024"],
        "cs2": np.concatenate([c2["cos2"], c2["sin2"]], 1),
        "rw": np.ascontiguousarray(np.concatenate(
            [i["w_router_group"][0], i["w_router_expert"][0].transpose(1, 0, 2).reshape(1024, 64)], 1)),
    }
    for n in ("w_in", "w_ssd_out", "w_attn_out", "w_out", "w_gate_e", "w_up_e", "w_down_e", "meta_tokens_2",
              "a_w_qkv_2", "a_w_o_2", "kv_w_2", "b_w_q_2", "b_w_o_2", "mlp_w_in_2", "mlp_w_out_2"):
        a[n] = np.ascontiguousarray(i[n])
    return a


def kernel(**inputs):
    from concourse import bacc
    from concourse.bass_utils import run_bass_kernel_spmd

    arrays = host_arrays({k: np.asarray(v) for k, v in inputs.items()})
    nc = bacc.Bacc("TRN2", target_bir_lowering=False, num_devices=1)
    d = {n: nc.dram_tensor(f"in_{n}", v.shape, mybir.dt.from_np(v.dtype), kind="ExternalInput").ap()
         for n, v in arrays.items()}
    out = nc.dram_tensor("out_0", (1, 512, 1024), F32, kind="ExternalOutput").ap()
    build(nc, d, out)
    r = run_bass_kernel_spmd(nc, [{f"in_{n}": v for n, v in arrays.items()}], core_ids=[0])
    return r.results[0]["out_0"]
```
